# Optimizing a Trainium2 kernel written in Bass

```python
import math
import jax
import jax.numpy as jnp
from jax import lax
import numpy as np
import jax, jax.numpy as jnp

D_MODEL = 1024
BATCH = 1
SEQ = 512
DEPTH = 1

N_MOD = 6
EPS = 1e-6
GM_CHUNK = 128
GM_HEAD = 128
GM_GROUPS = D_MODEL // GM_HEAD
GM_WIDTH = GM_GROUPS * GM_HEAD
SSM_INNER = 2 * D_MODEL
SSM_HEAD_DIM = 64
SSM_HEADS = SSM_INNER // SSM_HEAD_DIM
SSM_GROUPS = 8
SSM_STATE = 128
SSM_CONV = 4
SSM_CHUNK = 128
CONV_DIM = SSM_INNER + 2 * SSM_GROUPS * SSM_STATE
D_FF = 4 * D_MODEL
IN_SIZES = (GM_WIDTH, GM_WIDTH, SSM_INNER, CONV_DIM, SSM_HEADS, D_MODEL, D_MODEL)
IN_WIDTH = sum(IN_SIZES)


def _split_offsets(sizes):
    offs, acc = [], 0
    for s in sizes[:-1]:
        acc += s
        offs.append(acc)
    return offs

def rms_norm(x, w=None):
    xf = x.astype(jnp.float32)
    y = xf * lax.rsqrt(jnp.mean(jnp.square(xf), axis=-1, keepdims=True) + EPS)
    if w is not None:
        y = y * w.astype(jnp.float32)
    return y.astype(x.dtype)

def gated_group_rms_norm(y, z, w, groups):
    g = y.astype(jnp.float32) * jax.nn.silu(z.astype(jnp.float32))
    gs = g.reshape(*g.shape[:-1], groups, -1)
    gs = gs * lax.rsqrt(jnp.mean(jnp.square(gs), axis=-1, keepdims=True) + EPS)
    return (gs.reshape(g.shape) * w.astype(jnp.float32)).astype(y.dtype)

def sgu_branch(u, v, norm_w, ws, bs):
    b, s, _ = v.shape
    u = jax.nn.gelu(u)
    v = rms_norm(jax.nn.gelu(v), norm_w)
    vc = v.reshape(b, s // GM_CHUNK, GM_CHUNK, GM_GROUPS, GM_HEAD)
    causal = jnp.tril(jnp.ones((GM_CHUNK, GM_CHUNK), dtype=bool))
    ws_c = jnp.where(causal[None], ws, jnp.zeros_like(ws))
    sv = jnp.einsum('gij,bnjgd->bnigd', ws_c, vc) + bs.T[None, None, :, :, None]
    return u * sv.reshape(b, s, GM_WIDTH)

def ssd_scan(xs, dt, A, Bm, Cm):
    b, s, h, p = xs.shape
    g, n = Bm.shape[-2], Bm.shape[-1]
    hpg = h // g
    q = SSM_CHUNK
    nc = s // q

    def to_chunks(t):
        return jnp.swapaxes(t.reshape(b, nc, q, *t.shape[2:]), 0, 1)

    xdt = (xs.astype(jnp.float32) * dt[..., None]).reshape(b, s, g, hpg, p)
    a = (dt * A).reshape(b, s, g, hpg)
    causal = jnp.tril(jnp.ones((q, q), dtype=bool))

    def step(state, inp):
        x_c, a_c, B_c, C_c = inp
        cum = jnp.cumsum(a_c, axis=1)
        cum_t = jnp.moveaxis(cum, 1, -1)
        seg = cum_t[..., :, None] - cum_t[..., None, :]
        decay = jnp.exp(jnp.where(causal, seg, -jnp.inf))
        cb = jnp.einsum('bign,bjgn->bgij', C_c, B_c)
        y_intra = jnp.einsum('bgij,bghij,bjghp->bighp', cb, decay, x_c)
        y_inter = jnp.einsum('bign,bghpn->bighp', C_c, state) * jnp.exp(cum)[..., None]
        last = cum[:, -1]
        w_end = jnp.exp(last[:, None] - cum)
        new_state = state * jnp.exp(last)[..., None, None] + jnp.einsum(
            'bjgn,bjgh,bjghp->bghpn', B_c, w_end, x_c)
        return new_state, y_intra + y_inter

    state0 = jnp.zeros((b, g, hpg, p, n), jnp.float32)
    _, ys = lax.scan(step, state0, (to_chunks(xdt), to_chunks(a),
                                    to_chunks(Bm.astype(jnp.float32)),
                                    to_chunks(Cm.astype(jnp.float32))))
    return jnp.swapaxes(ys, 0, 1).reshape(b, s, h, p)

def ssd_branch(z, xbc, dt_raw, conv_w, conv_b, dt_bias, a_log, d_skip, norm_w):
    b, s, _ = xbc.shape
    xbc = lax.conv_general_dilated(
        xbc, conv_w[:, None, :], window_strides=(1,), padding=[(SSM_CONV - 1, 0)],
        dimension_numbers=('NWC', 'WIO', 'NWC'), feature_group_count=CONV_DIM) + conv_b
    xbc = jax.nn.silu(xbc)
    gn = SSM_GROUPS * SSM_STATE
    xs = xbc[..., :SSM_INNER].reshape(b, s, SSM_HEADS, SSM_HEAD_DIM)
    Bm = xbc[..., SSM_INNER:SSM_INNER + gn].reshape(b, s, SSM_GROUPS, SSM_STATE)
    Cm = xbc[..., SSM_INNER + gn:].reshape(b, s, SSM_GROUPS, SSM_STATE)
    dt = jax.nn.softplus(dt_raw.astype(jnp.float32) + dt_bias.astype(jnp.float32))
    A = -jnp.exp(a_log.astype(jnp.float32))
    y = ssd_scan(xs, dt, A, Bm, Cm)
    y = y + xs.astype(jnp.float32) * d_skip.astype(jnp.float32)[:, None]
    y = y.reshape(b, s, SSM_INNER).astype(z.dtype)
    return gated_group_rms_norm(y, z, norm_w, SSM_GROUPS)

def first_inputs(seed: int = 0) -> dict:
    key = jax.random.key(seed)
    ks = jax.random.split(key, 22)
    f = jnp.float32
    L = DEPTH

    def nrm(k, shape, fan_in):
        return jax.random.normal(k, shape, f) * (fan_in ** -0.5)

    x = jax.random.normal(ks[0], (BATCH, SEQ, D_MODEL), f)
    c = jax.random.normal(ks[1], (BATCH, D_MODEL), f)
    w_mod = 0.5 * nrm(ks[2], (L, D_MODEL, N_MOD * D_MODEL), D_MODEL)
    b_mod = 0.01 * jax.random.normal(ks[3], (L, N_MOD * D_MODEL), f)
    w_in = nrm(ks[4], (L, D_MODEL, IN_WIDTH), D_MODEL)
    gm_norm_w = 1.0 + 0.05 * jax.random.normal(ks[5], (L, GM_WIDTH), f)
    gm_ws = nrm(ks[6], (L, GM_GROUPS, GM_CHUNK, GM_CHUNK), GM_CHUNK)
    gm_bs = 1.0 + 0.1 * jax.random.normal(ks[7], (L, GM_GROUPS, GM_CHUNK), f)
    conv_w = nrm(ks[8], (L, SSM_CONV, CONV_DIM), SSM_CONV)
    conv_b = 0.01 * jax.random.normal(ks[9], (L, CONV_DIM), f)
    dt0 = jnp.exp(jax.random.uniform(ks[10], (L, SSM_HEADS), f,
                                     minval=math.log(1e-3), maxval=math.log(1e-1)))
    dt_bias = dt0 + jnp.log(-jnp.expm1(-dt0))
    a_log = jnp.log(jax.random.uniform(ks[11], (L, SSM_HEADS), f, minval=1.0, maxval=16.0))
    d_skip = 1.0 + 0.1 * jax.random.normal(ks[12], (L, SSM_HEADS), f)
    ssm_norm_w = 1.0 + 0.05 * jax.random.normal(ks[13], (L, SSM_INNER), f)
    w_branch_gm = nrm(ks[14], (L, GM_WIDTH, D_MODEL), GM_WIDTH)
    w_branch_ssm = nrm(ks[15], (L, SSM_INNER, D_MODEL), SSM_INNER)
    w_out = nrm(ks[16], (L, D_MODEL, D_MODEL), D_MODEL)
    w_ff1 = nrm(ks[17], (L, D_MODEL, D_FF), D_MODEL)
    w_ff2 = nrm(ks[18], (L, D_FF, D_MODEL), D_FF)
    final_norm_w = 1.0 + 0.05 * jax.random.normal(ks[19], (D_MODEL,), f)
    return {'x': x, 'c': c, 'w_mod': w_mod, 'b_mod': b_mod, 'w_in': w_in,
            'gm_norm_w': gm_norm_w, 'gm_ws': gm_ws, 'gm_bs': gm_bs,
            'conv_w': conv_w, 'conv_b': conv_b, 'dt_bias': dt_bias, 'a_log': a_log,
            'd_skip': d_skip, 'ssm_norm_w': ssm_norm_w, 'w_branch_gm': w_branch_gm,
            'w_branch_ssm': w_branch_ssm, 'w_out': w_out, 'w_ff1': w_ff1,
            'w_ff2': w_ff2, 'final_norm_w': final_norm_w}

def first_block(x, c, w_mod, b_mod, w_in, gm_norm_w, gm_ws, gm_bs, conv_w, conv_b,
              dt_bias, a_log, d_skip, ssm_norm_w, w_branch_gm, w_branch_ssm, w_out,
              w_ff1, w_ff2, final_norm_w):
    c_act = jax.nn.silu(c)
    offs = _split_offsets(IN_SIZES)
    for l in range(DEPTH):
        mod = (c_act @ w_mod[l] + b_mod[l])[:, None, :]
        sh1, sc1, g1, sh2, sc2, g2 = jnp.split(mod, N_MOD, axis=-1)
        h = rms_norm(x) * (1.0 + sc1) + sh1
        proj = h @ w_in[l]
        u, v, z, xbc, dt_raw, gate_a, gate_b = jnp.split(proj, offs, axis=-1)
        y_a = sgu_branch(u, v, gm_norm_w[l], gm_ws[l], gm_bs[l])
        y_b = ssd_branch(z, xbc, dt_raw, conv_w[l], conv_b[l], dt_bias[l], a_log[l],
                         d_skip[l], ssm_norm_w[l])
        mixed = (jax.nn.sigmoid(gate_a) * (y_a @ w_branch_gm[l])
                 + jax.nn.sigmoid(gate_b) * (y_b @ w_branch_ssm[l]))
        x = x + g1 * (mixed @ w_out[l])
        h2 = rms_norm(x) * (1.0 + sc2) + sh2
        x = x + g2 * (jnp.square(jax.nn.relu(h2 @ w_ff1[l])) @ w_ff2[l])
    return rms_norm(x, final_norm_w)


CHUNK = 64
D_MIX = D_MODEL
D_POOL = D_MIX // 2
POOL_WINDOWS = (2, 4, 8, 16)
N_POOL_GROUPS = len(POOL_WINDOWS)
POOL_GROUP = D_POOL // N_POOL_GROUPS
D_RWKV = D_MIX - D_POOL
RWKV_HEAD = 64
N_RWKV_HEADS = D_RWKV // RWKV_HEAD
DECAY_LORA = 64
AAA_LORA = 64
D_SHIFT = 3 * D_RWKV + DECAY_LORA + AAA_LORA
D_IN = 2 * D_POOL + D_SHIFT + D_RWKV
NORM_EPS = 1e-6
GN_EPS = 64e-5


def rmsnorm(x, gain):
    x32 = x.astype(jnp.float32)
    inv = lax.rsqrt(jnp.mean(x32 * x32, axis=-1, keepdims=True) + NORM_EPS)
    return (x32 * inv * gain.astype(jnp.float32)).astype(x.dtype)

def multi_scale_pool(u, pool_w, pool_scale):
    B, S, _ = u.shape
    u32 = u.astype(jnp.float32).reshape(B, S, N_POOL_GROUPS, POOL_GROUP)
    cs = jnp.cumsum(u32, axis=1)
    cs0 = jnp.concatenate([jnp.zeros_like(cs[:, :1]), cs], axis=1)
    pos = jnp.arange(S)
    outs = []
    for g, w in enumerate(POOL_WINDOWS):
        hi = cs[:, :, g]
        lo = jnp.concatenate([jnp.zeros((B, w - 1, POOL_GROUP), jnp.float32),
                              cs0[:, :S + 1 - w, g]], axis=1)
        cnt = jnp.minimum(pos + 1, w).astype(jnp.float32)[None, :, None]
        outs.append((hi - lo) / cnt - u32[:, :, g])
    pooled = jnp.stack(outs, axis=2)
    mixed = jnp.einsum('bsgc,gcd->bsgd', pooled, pool_w.astype(jnp.float32))
    return (mixed.reshape(B, S, D_POOL) * pool_scale.astype(jnp.float32)).astype(u.dtype)

def rwkv7_time_mix(feat, w0, w_up, a0, a_up, k_k, k_a, r_k, gn_gain, gn_bias):
    B, S, _ = feat.shape
    H, N = N_RWKV_HEADS, RWKV_HEAD
    f = feat.astype(jnp.float32)
    r = f[..., :D_RWKV]
    k = f[..., D_RWKV:2 * D_RWKV]
    v = f[..., 2 * D_RWKV:3 * D_RWKV]
    w_lr = f[..., 3 * D_RWKV:3 * D_RWKV + DECAY_LORA]
    a_lr = f[..., 3 * D_RWKV + DECAY_LORA:]
    ww = w0.astype(jnp.float32) + jnp.tanh(w_lr) @ w_up.astype(jnp.float32)
    decay = jnp.exp(-jnp.exp(-jax.nn.softplus(-ww) - 0.5))
    a = jax.nn.sigmoid(a0.astype(jnp.float32) + a_lr @ a_up.astype(jnp.float32))
    heads = lambda t: t.reshape(B, S, H, N)
    kk = heads(k * k_k.astype(jnp.float32))
    kk = kk / jnp.maximum(jnp.sqrt(jnp.sum(kk * kk, axis=-1, keepdims=True)), 1e-12)
    k = k * (1.0 + (a - 1.0) * k_a.astype(jnp.float32))
    r, k, v, decay, a = heads(r), heads(k), heads(v), heads(decay), heads(a)

    def step(state, inp):
        r_t, k_t, v_t, w_t, kk_t, a_t = inp
        sa = jnp.einsum('bhvk,bhk->bhv', state, -kk_t)
        state = (state * w_t[:, :, None, :]
                 + sa[..., None] * (kk_t * a_t)[:, :, None, :]
                 + v_t[..., None] * k_t[:, :, None, :])
        y_t = jnp.einsum('bhvk,bhk->bhv', state, r_t)
        return state, y_t

    tm = lambda t: jnp.moveaxis(t, 1, 0)
    state0 = jnp.zeros((B, H, N, N), jnp.float32)
    _, y = lax.scan(step, state0, (tm(r), tm(k), tm(v), tm(decay), tm(kk), tm(a)))
    y = jnp.moveaxis(y, 0, 1)
    mu = jnp.mean(y, axis=-1, keepdims=True)
    var = jnp.mean(jnp.square(y - mu), axis=-1, keepdims=True)
    y = (y - mu) * lax.rsqrt(var + GN_EPS)
    y = y * gn_gain.astype(jnp.float32).reshape(H, N) + gn_bias.astype(jnp.float32).reshape(H, N)
    bonus = jnp.sum(r * k * r_k.astype(jnp.float32), axis=-1, keepdims=True) * v
    return (y + bonus).reshape(B, S, D_RWKV)

def second_inputs(seed: int = 0) -> dict:
    key = jax.random.key(seed)
    ks = jax.random.split(key, 20)
    f32 = jnp.float32
    nrm = lambda k, shape, s: jax.random.normal(k, shape, f32) * s
    x = jax.random.normal(ks[0], (BATCH, SEQ, D_MODEL), f32)
    norm_gain = 1.0 + nrm(ks[1], (DEPTH, D_MODEL), 0.05)
    w_in = nrm(ks[2], (DEPTH, D_MODEL, D_IN), D_MODEL ** -0.5)
    pool_w = nrm(ks[3], (DEPTH, N_POOL_GROUPS, POOL_GROUP, POOL_GROUP), POOL_GROUP ** -0.5)
    pool_scale = 1.0 + nrm(ks[4], (DEPTH, D_POOL), 0.05)
    shift_mu = jax.random.uniform(ks[5], (DEPTH, D_SHIFT), f32, 0.0, 1.0)
    w0 = jax.random.uniform(ks[6], (DEPTH, D_RWKV), f32, -4.0, 2.0)
    w_up = nrm(ks[7], (DEPTH, DECAY_LORA, D_RWKV), 0.1)
    a0 = nrm(ks[8], (DEPTH, D_RWKV), 0.1)
    a_up = nrm(ks[9], (DEPTH, AAA_LORA, D_RWKV), 0.5 * AAA_LORA ** -0.5)
    k_k = 0.85 + nrm(ks[10], (DEPTH, D_RWKV), 0.05)
    k_a = 1.0 + nrm(ks[11], (DEPTH, D_RWKV), 0.05)
    r_k = nrm(ks[12], (DEPTH, N_RWKV_HEADS, RWKV_HEAD), 0.1)
    gn_gain = 1.0 + nrm(ks[13], (DEPTH, D_RWKV), 0.05)
    gn_bias = nrm(ks[14], (DEPTH, D_RWKV), 0.02)
    w_out = nrm(ks[15], (DEPTH, D_MIX, D_MODEL), D_MIX ** -0.5)
    final_gain = 1.0 + nrm(ks[16], (D_MODEL,), 0.05)
    return {"x": x, "norm_gain": norm_gain, "w_in": w_in, "pool_w": pool_w,
            "pool_scale": pool_scale, "shift_mu": shift_mu, "w0": w0, "w_up": w_up,
            "a0": a0, "a_up": a_up, "k_k": k_k, "k_a": k_a, "r_k": r_k,
            "gn_gain": gn_gain, "gn_bias": gn_bias, "w_out": w_out, "final_gain": final_gain}

def second_block(x, norm_gain, w_in, pool_w, pool_scale, shift_mu, w0, w_up, a0, a_up,
              k_k, k_a, r_k, gn_gain, gn_bias, w_out, final_gain):
    for l in range(DEPTH):
        h = rmsnorm(x, norm_gain[l])
        z = h @ w_in[l]
        u_a = z[..., :D_POOL]
        g_a = z[..., D_POOL:2 * D_POOL]
        sh = z[..., 2 * D_POOL:2 * D_POOL + D_SHIFT]
        g_b = z[..., 2 * D_POOL + D_SHIFT:]
        sh_prev = jnp.pad(sh, ((0, 0), (1, 0), (0, 0)))[:, :-1]
        sh = sh + shift_mu[l] * (sh_prev - sh)
        y_a = multi_scale_pool(u_a, pool_w[l], pool_scale[l])
        y_b = rwkv7_time_mix(sh, w0[l], w_up[l], a0[l], a_up[l], k_k[l], k_a[l],
                             r_k[l], gn_gain[l], gn_bias[l]).astype(x.dtype)
        y = jnp.concatenate([y_a * jax.nn.silu(g_a), y_b * jax.nn.silu(g_b)], axis=-1)
        x = x + y @ w_out[l]
    return rmsnorm(x, final_gain)


def setup_inputs(seed=0):
    out = dict(first_inputs(seed))
    for name, value in second_inputs(seed + 1).items():
        if name != "x":
            out[name + "_2"] = value
    return out


def reference(
    x, c, w_mod, b_mod, w_in, gm_norm_w, gm_ws, gm_bs, conv_w, conv_b, dt_bias, a_log, d_skip,
    ssm_norm_w, w_branch_gm, w_branch_ssm, w_out, w_ff1, w_ff2, final_norm_w, norm_gain_2,
    w_in_2, pool_w_2, pool_scale_2, shift_mu_2, w0_2, w_up_2, a0_2, a_up_2, k_k_2, k_a_2, r_k_2,
    gn_gain_2, gn_bias_2, w_out_2, final_gain_2,
):
    x = first_block(
        x, c, w_mod, b_mod, w_in, gm_norm_w, gm_ws, gm_bs, conv_w, conv_b, dt_bias, a_log,
        d_skip, ssm_norm_w, w_branch_gm, w_branch_ssm, w_out, w_ff1, w_ff2, final_norm_w,
    )
    return second_block(
        x, norm_gain_2, w_in_2, pool_w_2, pool_scale_2, shift_mu_2, w0_2, w_up_2, a0_2, a_up_2,
        k_k_2, k_a_2, r_k_2, gn_gain_2, gn_bias_2, w_out_2, final_gain_2,
    )


_drawn_inputs = setup_inputs


def setup_inputs(seed=0):
    import zlib

    import numpy as np

    out = dict(_drawn_inputs(seed))
    spreads = {}
    factors = {'b_mod': 2.683,
     'gm_norm_w': 8.0,
     'gm_bs': 3.859,
     'conv_b': 8.0,
     'd_skip': 5.315,
     'ssm_norm_w': 5.3,
     'pool_scale_2': 3.527,
     'a0_2': 3.133,
     'k_k_2': 6.323,
     'gn_gain_2': 3.035,
     'gn_bias_2': 7.32}
    for name, (base, spread) in spreads.items():
        noise = np.random.default_rng([zlib.crc32(name.encode()), seed]).standard_normal(out[name].shape)
        drawn = base * np.exp(spread * noise) if base else spread * noise
        out[name] = jnp.asarray(drawn.astype(out[name].dtype))
    for name, factor in factors.items():
        out[name] = (out[name] * factor).astype(out[name].dtype)
    return out
```

```python
from contextlib import ExitStack

import concourse.bass as bass
from concourse import mybir

F32 = mybir.dt.float32
F32R = mybir.dt.float32r
BF16 = mybir.dt.bfloat16
U32 = mybir.dt.uint32
ALU = mybir.AluOpType
ACTF = mybir.ActivationFunctionType
AX_X = mybir.AxisListType.X

P = 128
EM05 = 0.6065306597126334
T = 512
NC = 4
D = 1024
KT = 8
NRAW = 3
NHL = 3
NEG = -1.0e30
BLOCKS = (1, 2)
ORDER2 = [("k", 0), ("r", 0), ("v", 0),
          ("k", 1), ("r", 1), ("gb", 0), ("ua", 0), ("ga", 0), ("v", 1),
          ("k", 2), ("r", 2), ("gb", 1), ("ua", 1), ("ga", 1), ("v", 2),
          ("k", 3), ("r", 3), ("gb", 2), ("ua", 2), ("ga", 2), ("v", 3),
          ("gb", 3), ("ua", 3), ("ga", 3)]




class Queue:

    def __init__(self, eng, sem):
        self.eng, self.sem, self.n, self.seen = eng, sem, 0, {}

    def wait(self, *tokens):
        for t in tokens:
            if t is not None and self.seen.get(id(t[0]), 0) < t[1]:
                self.seen[id(t[0])] = t[1]
                self.eng.wait_ge(t[0], t[1])

    def op(self, fn, *tokens):
        self.wait(*tokens)
        self.n += 1
        fn(self.eng).then_inc(self.sem, 1)
        return (self.sem, self.n)

    def quiet(self, fn, *tokens):
        self.wait(*tokens)
        fn(self.eng)

    def dma(self, fn, sem, value, *tokens):
        self.wait(*tokens)
        fn(self.eng).then_inc(sem, 16)
        return (sem, value)


class Buf:

    def __init__(self, t):
        self.t, self.free, self.sem, self.uses = t, [], None, 0

    def __getitem__(self, k):
        return self.t[k]


class Stock:

    def __init__(self, bufs):
        self.bufs = list(bufs)

    def get(self):
        return self.bufs.pop(0)

    def give(self, b, *tokens):
        b.free = list(tokens)
        self.bufs.append(b)


class Ring:
    def __init__(self, bufs):
        self.bufs, self.i = bufs, 0

    def next(self):
        b = self.bufs[self.i % len(self.bufs)]
        self.i += 1
        return b


def build_program(nc, A, out, blocks=(1, 2)):
    ctx = ExitStack()
    with ctx:
        def sb(name, shape, dt=F32, c=ctx):
            return c.enter_context(nc.sbuf_tensor(name, shape, dt))

        def sem(name):
            return ctx.enter_context(nc.semaphore(name))

        PE, ACT, DVE, POOL, SP = (
            Queue(e, sem(f"s_{n}")) for n, e in (("pe", nc.tensor), ("act", nc.scalar), ("dve", nc.vector),
                                                 ("pool", nc.gpsimd), ("sp", nc.sync)))

        XT = sb("XT", [P, KT, T])
        ident = sb("ident", [P, P])
        ones = sb("ones", [P, P])
        triu = sb("triu", [P, P])
        identb = sb("identb", [P, P], BF16)
        maskb = sb("maskb", [P, P], BF16)
        pcA = sb("pcA", [P, 128])
        pcB = sb("pcB", [P, 128])
        pcC = sb("pcC", [P, 64])
        modc = sb("modc", [P, 48])
        opc = sb("opc", [P, 16])
        small = sb("small", [P, 64])
        cact = sb("cact", [P, 8])
        raw = [Buf(sb(f"raw{i}", [P, KT, 128])) for i in range(NRAW)]
        for i, b in enumerate(raw):
            b.sem = sem(f"s_raw{i}")
        whi = [sb(f"whi{i}", [P, KT, 128], F32R) for i in range(NHL)]
        wlo = [sb(f"wlo{i}", [P, KT, 128], F32R) for i in range(NHL)]
        wfree = [[] for _ in range(NHL)]
        Hh = sb("Hh", [P, KT, T], F32R)
        Hl = sb("Hl", [P, KT, T], F32R)
        tmp = Ring([Buf(sb(f"tmp{i}", [P, T])) for i in range(3)])
        acc = Buf(sb("acc", [P, T]))
        rb = Buf(sb("rb", [P, T]))

        def region(kb, *tensors):
            with ExitStack() as c:
                if kb:
                    sb(f"pad_{tensors[0][0]}", [P, kb * 256], F32, c)
                return [sb(*t, c=c) for t in tensors]

        BK = [Buf(ctx.enter_context(nc.psum_tensor(f"bk{i}", [P, T], F32))) for i in range(8)]
        MB = Ring(BK[0:3])

        plan = []

        def cols(w, c0, n=128, k0=0, kt=KT):
            return w[k0 * 128:(k0 + kt) * 128, c0:c0 + n].rearrange("(k p) n -> p k n", p=P)

        W_IN, W_MOD = A["w_in"][0], A["w_mod"][0]
        OFF = dict(u=0, v=1024, z=2048, x=4096, b=6144, c=7168, dt=8192, ga=8224, gb=9248)

        def add(kind, ap, n=128):
            plan.append((kind, ap, n))

        if 1 in blocks:
            add("w", cols(W_IN, OFF["dt"], 32), 32)
            for g in range(8):
                for m, c0 in enumerate((OFF["x"] + g * 256, OFF["x"] + g * 256 + 128, OFF["b"] + g * 128,
                                        OFF["c"] + g * 128)):
                    add("w", cols(W_IN, c0))
                    add("mod", cols(W_MOD, (16 + 4 * g + m) * 128))
                for c0 in (OFF["z"] + g * 256, OFF["z"] + g * 256 + 128):
                    add("w", cols(W_IN, c0))
            for m in range(8):
                add("w", cols(W_IN, OFF["v"] + m * 128))
            for m in range(8):
                add("w", cols(W_IN, OFF["u"] + m * 128))
            for m in range(8):
                add("w", cols(W_IN, OFF["ga"] + m * 128))
            for m in range(8):
                add("w", cols(W_IN, OFF["gb"] + m * 128))
            for m in range(8):
                add("w", cols(A["w_branch_gm"][0], m * 128))
            for m in range(8):
                add("w", cols(A["w_branch_ssm"][0], m * 128, k0=8))
            for m in range(8):
                add("w", cols(A["w_branch_ssm"][0], m * 128))
            for m in range(8):
                add("w", cols(A["w_out"][0], m * 128))
            for f in range(2):
                for m in range(16):
                    add("w", cols(A["w_ff1"][0], (f * 16 + m) * 128))
                for m in range(8):
                    add("w", cols(A["w_ff2"][0], m * 128, k0=16 * f))
                    add("w", cols(A["w_ff2"][0], m * 128, k0=16 * f + 8))
        W2 = A["w_in_2"][0]
        OFF2 = dict(ua=0, ga=512, r=1024, k=1536, v=2048, lr=2560, gb=2688)
        if 2 in blocks:
            add("w", cols(W2, OFF2["lr"]))
            for n, m in ORDER2:
                add("w", cols(W2, OFF2[n] + m * 128))
            for m in range(8):
                add("w", cols(A["w_out_2"][0], m * 128, kt=7))
            add("w", A["w_out_2"][0][7 * 128:8 * 128, :].rearrange("p (m n) -> p m n", n=P))

        st = dict(load=0, prep=0, use=0, hl=0)
        ready, slots = {}, {}

        def load():
            i = st["load"]
            st["load"] += 1
            kind, ap, n = plan[i]
            b = raw[i % NRAW]
            kt = ap.shape[1]
            SP.dma(lambda e, b=b, ap=ap, n=n: e.dma_start(b.t[:, 0:kt, 0:n], ap), b.sem, 16 * (i // NRAW + 1), *b.free)

        def prep():
            i = st["prep"]
            st["prep"] += 1
            kind, ap, n = plan[i]
            b = raw[i % NRAW]
            landed = (b.sem, 16 * (i // NRAW + 1))
            if kind == "mod":
                ready[i] = landed
                return
            s = st["hl"] % NHL
            st["hl"] += 1
            slots[i] = s
            kt = ap.shape[1]
            th = ACT.op(lambda e: e.activation(whi[s][:, 0:kt, 0:n], b.t[:, 0:kt, 0:n], ACTF.Copy), landed, *wfree[s])
            tl = DVE.op(lambda e: e.tensor_tensor(wlo[s][:, 0:kt, 0:n], b.t[:, 0:kt, 0:n],
                                                  whi[s][:, 0:kt, 0:n].bitcast(F32), ALU.subtract),
                        landed, th, *wfree[s])
            ready[i] = (th, tl)
            b.free = [tl]

        def take(kind):
            i = st["use"]
            st["use"] += 1
            assert plan[i][0] == kind
            ahead = i + 1
            while True:
                while st["prep"] <= i:
                    while st["load"] <= st["prep"]:
                        load()
                    prep()
                if st["prep"] < len(plan) and st["prep"] <= i + 2:
                    nxt = st["prep"]
                    while st["load"] <= nxt:
                        load()
                    prep()
                    continue
                break
            while st["load"] < len(plan):
                before = st["load"] - NRAW
                if before >= (i if plan[before][0] == "mod" else st["prep"]):
                    break
                load()
            return i, slots.get(i)

        def release(i, tok):
            if plan[i][0] == "mod":
                raw[i % NRAW].free = [tok]
            else:
                wfree[slots[i]] = [tok]

        def gemm(X_h, X_l, xtok, nchunk=1, hook=None, every=1, kt=KT):
            bk = MB.next()
            PE.wait(*bk.free)
            for c in range(nchunk):
                i, s = take("w")
                PE.wait(*ready[i])
                for k in range(kt):
                    kk = c * KT + k
                    PE.wait(*xtok[kk])
                    for w, x in ((whi, X_h), (whi, X_l), (wlo, X_h)):
                        first = kk == 0 and w is whi and x is X_h
                        last = kk == (nchunk - 1) * KT + kt - 1 and w is wlo
                        fn = lambda e, w=w, x=x, k=k, kk=kk, first=first, last=last, s=s: e.matmul(
                            bk.t[:, :], w[s][:, k, :], x[:, kk, :], start=first, stop=last)
                        if k == kt - 1 and w is wlo:
                            tok = PE.op(fn)
                        else:
                            PE.quiet(fn)
                    if hook and k % every == every - 1:
                        hook()
                release(i, tok)
            return bk, tok

        tz = POOL.op(lambda e: e.memset(ident[:, :], 0.0))
        t_id = POOL.op(lambda e: e.affine_select(out=ident[:, :], in_=ident[:, :], compare_op=ALU.not_equal, fill=1.0,
                                                 base=0, pattern=[[-1, P]], channel_multiplier=1), tz)
        t_ones = POOL.op(lambda e: e.memset(ones[:, :], 1.0))
        t_triu = POOL.op(lambda e: e.affine_select(out=triu[:, :], in_=ones[:, :], compare_op=ALU.is_ge, fill=0.0,
                                                   base=0, pattern=[[1, P]], channel_multiplier=-1), t_ones)
        t_idb = POOL.op(lambda e: e.tensor_copy(identb[:, :], ident[:, :]), t_id)
        tz = POOL.op(lambda e: e.memset(maskb[:, :], 0.0))
        t_mask = POOL.op(lambda e: e.affine_select(out=maskb[:, :], in_=maskb[:, :], compare_op=ALU.is_ge, fill=NEG,
                                                   base=0, pattern=[[1, P]], channel_multiplier=-1), tz)

        s_par = sem("s_par")
        s_fin = [sem("s_out0"), sem("s_out1")]
        par = {}

        v = lambda name: A[name].rearrange("a (n p) -> (a n) p", p=P)
        v1 = lambda name: A[name].rearrange("(n p) -> n p", p=P)
        rows, where = [], {}

        pr = region(64, *((f"pr{i}", [P, P]) for i in range(3)))

        def put(tile, r, name, ap, n):
            SP.dma(lambda e: e.dma_start(pr[tile][r:r + n, :], ap), s_par, 0)
            where[name] = (tile, r)
            return r + n

        s_x = sem("s_x")
        xnat, xs = region(0, ("xnat", [P, NC, D]), ("xs", [P, NC, D]))
        r = 0
        for name, ap, n in (("c", v("c"), 8), ("b_mod", v("b_mod"), 48), ("conv_b", v("conv_b"), 32),
                            ("gm_norm_w", v("gm_norm_w"), 8), ("ssm_norm_w", v("ssm_norm_w"), 16),
                            ("final_norm_w", v1("final_norm_w"), 8), ("norm_gain_2", v("norm_gain_2"), 8)):
            r = put(1, r, name, ap, n)
        t_par = (s_par, 16 * 7)
        for c in range(NC):
            SP.dma(lambda e, c=c: e.dma_start(xnat[:, c, :], A["x"][0, c * 128:(c + 1) * 128, :]), s_x, 0)
        t_x = (s_x, 64)
        if 1 in blocks:
            wm = region(32, *((f"wm{i}", [P, KT, 256]) for i in range(4)))
            wm += region(73, *((f"wm{i}", [P, KT, 256]) for i in range(4, 8)))
            s_wm = [sem(f"s_wm{i}") for i in range(8)]
            for i in range(8):
                SP.dma(lambda e, i=i: e.dma_start(wm[i][:, :, :], cols(W_MOD, i * 256, 256)), s_wm[i], 16)
        s_par2 = sem("s_par2")
        s_par, s_par0 = s_par2, s_par
        put(0, 0, "conv_w", A["conv_w"].rearrange("a k (n p) -> (a k n) p", p=P), 128)
        r = 0
        for name, ap, n in (("pool_scale_2", v("pool_scale_2"), 4), ("shift_mu_2", v("shift_mu_2"), 13),
                            ("w0_2", v("w0_2"), 4), ("a0_2", v("a0_2"), 4), ("k_k_2", v("k_k_2"), 4),
                            ("k_a_2", v("k_a_2"), 4),
                            ("r_k_2", A["r_k_2"].rearrange("a (n q) d -> (a n) (q d)", q=2), 4),
                            ("gn_gain_2", v("gn_gain_2"), 4), ("gn_bias_2", v("gn_bias_2"), 4),
                            ("final_gain_2", v1("final_gain_2"), 8)):
            r = put(2, r, name, ap, n)
        rC = r
        tp = []

        def turn(i, dst, n, tok, scale=1.0):
            tm = PE.op(lambda e: e.transpose(BK[i].t[:, 0:n], pr[i][0:n, :], ident[0:n, 0:n]), tok, t_id)
            tp.append(DVE.op(lambda e: e.tensor_scalar(dst[:, 0:n], BK[i].t[:, 0:n], scale, None, ALU.mult), tm))
            BK[i].free = [tp[-1]]

        turn(1, pcB, 128, t_par)
        t_pb = tp[0]
        cw = lambda tap, tile: pcA[:, tap * 32 + tile:tap * 32 + tile + 1]

        def col(name, m):
            tile, r0 = where[name]
            return (pcA, pcB, pcC)[tile][:, r0 + m:r0 + m + 1]

        def colr(name, m, n):
            tile, r0 = where[name]
            return (pcA, pcB, pcC)[tile][:, r0 + m:r0 + m + n]

        t_eps = DVE.op(lambda e: e.memset(small[:, 0:1], 1e-6))
        t_eps = DVE.op(lambda e: e.memset(small[:, 1:2], 64e-5))
        EPS, GEPS = small[:, 0:1], small[:, 1:2]


        def square_sum(m, src, tok, prev):
            if m == 0:
                return DVE.op(lambda e: e.tensor_tensor(acc[:, :], src, src, ALU.mult), tok, *acc.free)
            b = tmp.next()
            t1 = ACT.op(lambda e: e.activation(b[:, :], src, ACTF.Square), tok, *b.free)
            t2 = DVE.op(lambda e: e.tensor_tensor(acc[:, :], acc[:, :], b[:, :], ALU.add), t1, prev)
            b.free = [t2]
            return t2

        def rstd_all(tok):
            bk = MB.next()
            tm = PE.op(lambda e: e.matmul(bk[:, :], ones[:, :], acc[:, :], start=True, stop=True), tok, t_ones, *bk.free)
            acc.free = [tm]
            ts = ACT.op(lambda e: e.activation(rb[:, :], bk[:, :], ACTF.Sqrt, bias=EPS, scale=1.0 / D), tm, t_eps, *rb.free)
            bk.free = [ts]
            return DVE.op(lambda e: e.reciprocal(rb[:, :], rb[:, :]), ts)

        def split(src, tok, hi, lo, hfree=()):
            th = ACT.op(lambda e: e.activation(hi, src, ACTF.Copy), tok, *hfree)
            tl = DVE.op(lambda e: e.tensor_tensor(lo, src, hi.bitcast(F32), ALU.subtract), th, tok, *hfree)
            return (th, tl)

        def norm_split(m, xsrc, xtok, rtok, scale, bias, stok, hfree):
            b = tmp.next()
            t1 = DVE.op(lambda e: e.tensor_tensor(b[:, :], xsrc, rb[:, :], ALU.mult), xtok, rtok, *b.free)
            if bias is None:
                t2 = ACT.op(lambda e: e.activation(b[:, :], b[:, :], ACTF.Copy, scale=scale), t1, stok)
            else:
                t2 = ACT.op(lambda e: e.activation(b[:, :], b[:, :], ACTF.Identity, scale=scale, bias=bias), t1, stok)
            th, tl = split(b[:, :], t2, Hh[:, m, :], Hl[:, m, :], hfree)
            b.free = [tl, th]
            return (th, tl)

        done = object()
        xt_tok = [None] * KT

        if 1 in blocks:
            YB, = region(0, ("YB", [P, 16, T]))
            V, = region(32, ("V", [P, NC, D]))
            f2 = region(48, *((f"cfb{j}", [P, T]) for j in range(6)))
            YA, = region(48, ("YA", [P, KT, T]))
            (bsb, dts, bc, *stemps) = region(
                64, ("bsb", [P, KT, P]), ("dts", [P, 8, P]), ("bc", [P, 3, 32]),
                *((f"cfa{j}", [P, T]) for j in range(6)),
                *((f"xr{i}", [P, T + 3]) for i in range(2)),
                *((f"dec{i}", [P, T]) for i in range(2)),
                *((f"xdt{i}", [P, 256]) for i in range(2)),
                *((f"xd{i}", [P, 256]) for i in range(2)),
                *((f"xw{i}", [P, 256]) for i in range(2)),
                *((f"bn{i}", [P, 128]) for i in range(2)),
                ("yv", [P, NC, 256]), ("state", [P, 256]))
            wsT, wraw = region(74, ("wsT", [P, KT, P]), ("wraw", [P, KT, P]))
            GA, = region(82, ("GA", [P, KT, T]))
            GB, = region(32, ("GB", [P, KT, T]))
            R2h, R2l = region(48, ("R2h", [P, KT, T], F32R), ("R2l", [P, KT, T], F32R))
            YBh, YBl = region(0, ("YBh", [P, 16, T], F32R), ("YBl", [P, 16, T], F32R))

            sq_t = []
            for c in range(NC):
                t = ACT.op(lambda e, c=c: e.activation(xs[:, c, :], xnat[:, c, :], ACTF.Square,
                                                       accum_out=small[:, 4 + c:5 + c]), t_x)
                sq_t.append(t)
            ts = ACT.op(lambda e: e.activation(small[:, 4:8], small[:, 4:8], ACTF.Sqrt, bias=EPS, scale=1.0 / D),
                        sq_t[-1], t_eps)
            ts = DVE.op(lambda e: e.reciprocal(small[:, 4:8], small[:, 4:8]), ts)
            for c in range(NC):
                t_xs = DVE.op(lambda e, c=c: e.tensor_scalar(xs[:, c, :], xnat[:, c, :], small[:, 4 + c:5 + c], None,
                                                             ALU.mult), ts)
        t_pc = t_pb
        if 1 not in blocks:
            turn(2, pcC, rC, (s_par, 16 * 11))
            t_pc = tp[-1]
            tm = None
        if 1 in blocks:
            t_c = ACT.op(lambda e: e.activation(cact[:, :], colr("c", 0, 8), ACTF.Silu), t_pb)
        for m in range(KT):
            bk = BK[3 + m % 2]
            for c in range(NC):
                tm = PE.op(lambda e, m=m, c=c, bk=bk: e.transpose(bk[:, c * 128:(c + 1) * 128],
                                                                 xnat[:, c, m * 128:(m + 1) * 128], ident[:, :]),
                           t_x, t_id, *bk.free)
            xt_tok[m] = ACT.op(lambda e, m=m, bk=bk: e.activation(XT[:, m, :], bk[:, :], ACTF.Copy), tm)
            bk.free = [xt_tok[m]]
        t_xt = xt_tok[KT - 1]
        t_later = (s_par, 16 * 11)

        def mods(n, m0):
            bk = MB.next()
            for m in range(m0, m0 + n):
                i, _ = take("mod")
                PE.wait(ready[i], t_c, *bk.free)
                for k in range(KT):
                    fn = lambda e, k=k, i=i, m=m: e.matmul(bk[:, m:m + 1], raw[i % NRAW].t[:, k, :], cact[:, k:k + 1],
                                                           start=(k == 0), stop=(k == KT - 1))
                    if k == KT - 1:
                        tm = PE.op(fn)
                    else:
                        PE.quiet(fn)
                release(i, tm)
            t = DVE.op(lambda e: e.tensor_tensor(modc[:, m0:m0 + n], bk[:, m0:m0 + n], colr("b_mod", m0, n), ALU.add),
                       tm, t_pb)
            bk.free = [t]
            return t

        if 1 in blocks:
            MOD = dict(sh1=0, sc1=8, g1=16, sh2=24, sc2=32, g2=40)
            bk = BK[7]
            for m in range(16):
                for k in range(KT):
                    fn = lambda e: e.matmul(bk[:, m:m + 1], wm[m // 2][:, k, (m % 2) * 128:(m % 2) * 128 + 128],
                                            cact[:, k:k + 1], start=(k == 0), stop=(k == KT - 1))
                    tm = PE.op(fn, (s_wm[m // 2], 16), t_c)
            t_mod = DVE.op(lambda e: e.tensor_tensor(modc[:, 0:16], bk[:, 0:16], colr("b_mod", 0, 16), ALU.add), tm, t_pb)
            bk.free = [t_mod]
            t_wmdead = tm
            t_op = DVE.op(lambda e: e.tensor_scalar(opc[:, 0:8], modc[:, 8:16], 1.0, None, ALU.add), t_mod)
            htok = [None] * KT
            for m in range(KT):
                bk = BK[5 + m % 2]
                for c in range(NC):
                    tm = PE.op(lambda e, m=m, c=c, bk=bk: e.transpose(bk[:, c * 128:(c + 1) * 128],
                                                                     xs[:, c, m * 128:(m + 1) * 128], ident[:, :]),
                               t_xs, *bk.free)
                b = tmp.next()
                t1 = ACT.op(lambda e, m=m, bk=bk, b=b: e.activation(b[:, :], bk[:, :], ACTF.Identity,
                                                                   scale=opc[:, m:m + 1], bias=modc[:, m:m + 1]),
                            tm, t_op, *b.free)
                bk.free = [t1]
                htok[m] = split(b[:, :], t1, Hh[:, m, :], Hl[:, m, :])
                b.free = [*htok[m]]
            t_xdead = tm
            turn(0, pcA, 128, t_later, 0.5)
            turn(2, pcC, rC, t_later)
            t_cb = DVE.op(lambda e: e.tensor_scalar(colr("conv_b", 0, 32), colr("conv_b", 0, 32), 0.5, None, ALU.mult), t_pb)
            t_pc = tp[-1]

            s_bc = sem("s_bc")
            for i, name in enumerate(("dt_bias", "a_log", "d_skip")):
                SP.dma(lambda e, i=i, name=name: e.dma_start(bc[:, i, :], A[name].to_broadcast([P, 32])), s_bc, 0)
            SP.dma(lambda e: e.dma_start(bsb[:, :, :], A["gm_bs"].rearrange("a g i -> a (g i)").to_broadcast([P, D])
                                         .rearrange("p (g i) -> p g i", g=KT)), s_bc, 0, *tp)
            t_bc = (s_bc, 64)
            DT, AA, CU, NCU, EC, WE, EL, SC = (dts[:, i, :] for i in range(8))
            i, s = take("w")
            bk = MB.next()
            PE.wait(*ready[i], *bk.free)
            for c in range(NC):
                for k in range(KT):
                    PE.wait(*htok[k])
                    for x, w in ((Hh, whi), (Hh, wlo), (Hl, whi)):
                        fn = lambda e, x=x, w=w, k=k, c=c, s=s, bk=bk: e.matmul(
                            bk[:, c * 32:(c + 1) * 32], x[:, k, c * 128:(c + 1) * 128], w[s][:, k, 0:32],
                            start=(k == 0 and x is Hh and w is whi), stop=(k == KT - 1 and x is Hl))
                        if c == NC - 1 and k == KT - 1 and x is Hl:
                            tm = PE.op(fn)
                        else:
                            PE.quiet(fn)
            release(i, tm)
            c4 = lambda ap: ap.rearrange("p (c h) -> p c h", c=NC)
            bcast = lambda i: bc[:, i, :].unsqueeze(1).to_broadcast([P, NC, 32])
            t = DVE.op(lambda e: e.tensor_tensor(c4(SC), c4(bk[:, 0:128]), bcast(0), ALU.add), tm, t_bc)
            bk.free = [t]
            t_al = ACT.op(lambda e: e.activation(bc[:, 1, :], bc[:, 1, :], ACTF.Exp), t_bc)
            t1 = ACT.op(lambda e: e.activation(DT, SC, ACTF.Abs), t)
            t1 = ACT.op(lambda e: e.activation(DT, DT, ACTF.Exp, scale=-1.0), t1)
            tu = DVE.op(lambda e: e.tensor_scalar(CU, DT, 1.0, None, ALU.add), t1)
            tl = ACT.op(lambda e: e.activation(AA, CU, ACTF.Ln), tu)
            td = DVE.op(lambda e: e.tensor_scalar(CU, CU, 1.0, None, ALU.subtract), tu, tl)
            tq = DVE.op(lambda e: e.tensor_scalar(NCU, CU, 0.0, None, ALU.is_equal), td)
            t2 = DVE.op(lambda e: e.tensor_tensor(AA, AA, NCU, ALU.add), tq, tl)
            t3 = DVE.op(lambda e: e.tensor_tensor(CU, CU, NCU, ALU.add), tq)
            t3 = DVE.op(lambda e: e.reciprocal(CU, CU), t3)
            t4 = DVE.op(lambda e: e.tensor_tensor(AA, AA, CU, ALU.mult), t2, t3)
            t4 = DVE.op(lambda e: e.tensor_tensor(AA, AA, DT, ALU.mult), t4)
            t_dt = DVE.op(lambda e: e.scalar_tensor_tensor(out=DT, in0=SC, scalar=0.0, in1=AA, op0=ALU.max, op1=ALU.add), t4)
            t5 = DVE.op(lambda e: e.scalar_tensor_tensor(out=c4(AA), in0=c4(DT), scalar=-1.0, in1=bcast(1),
                                                         op0=ALU.mult, op1=ALU.mult), t_dt, t_al)
            bk = BK[7]
            tm = PE.op(lambda e: e.matmul(bk[:, 0:128], triu[:, :], AA, start=True, stop=True), t5, t_triu, *bk.free)
            tm = PE.op(lambda e: e.matmul(bk[:, 128:256], ones[:, :], AA, start=True, stop=True))
            t6 = ACT.op(lambda e: e.activation(EC, bk[:, 0:128], ACTF.Exp), tm)
            t6 = ACT.op(lambda e: e.activation(EL, bk[:, 128:256], ACTF.Exp), tm)
            t7 = DVE.op(lambda e: e.tensor_scalar(NCU, bk[:, 0:128], -1.0, None, ALU.mult), tm, t6)
            t8 = DVE.op(lambda e: e.tensor_tensor(WE, bk[:, 128:256], NCU, ALU.add), t7)
            bk.free = [t8]
            t9 = ACT.op(lambda e: e.activation(WE, WE, ACTF.Exp), t8)
            t_dec = [t_dt, t5, t7, t9]

            it = iter([Buf(t) for t in stemps])
            take_n = lambda n: [next(it) for _ in range(n)]
            cf = [take_n(6), [Buf(t) for t in f2]]
            xr, dec, xdt, xd, xw, bn = (Ring(take_n(2)) for _ in range(6))
            ca = tmp
            yv, state = take_n(2)
            for b in xr.bufs:
                t_xr0 = DVE.op(lambda e, b=b: e.memset(b[:, 0:3], 0.0))

            def conv(bk, tm, tile, dst):
                b, a = xr.next(), ca.next()
                t1 = ACT.op(lambda e: e.activation(b[:, 3:T + 3], bk[:, :], ACTF.Copy), tm, *b.free)
                t2 = ACT.op(lambda e: e.activation(a[:, :], bk[:, :], ACTF.Identity, scale=cw(3, tile),
                                                   bias=col("conv_b", tile)), tm, t_pc, t_cb, *a.free)
                bk.free = [t2]
                for tap in range(3):
                    t2 = DVE.op(lambda e, tap=tap: e.scalar_tensor_tensor(
                        out=a[:, :], in0=b[:, tap:tap + T], scalar=cw(tap, tile), in1=a[:, :],
                        op0=ALU.mult, op1=ALU.add), t1, t2, t_xr0)
                b.free = [t2]
                q = tmp.next()
                t3 = ACT.op(lambda e: e.activation(q[:, :], a[:, :], ACTF.Tanh), t2, *q.free)
                t3 = DVE.op(lambda e: e.scalar_tensor_tensor(out=dst[:, :], in0=q[:, :], scalar=1.0, in1=a[:, :],
                                                             op0=ALU.add, op1=ALU.mult), t3, *dst.free)
                a.free = q.free = [t3]
                return t3

            def ssd(g, F, ft):
                h4 = lambda ap: ap.rearrange("p (h d) -> p h d", h=4)
                colh = lambda ap, c: ap[:, c * 32 + g * 4:c * 32 + g * 4 + 4].unsqueeze(2).to_broadcast([P, 4, 64])
                ytok = []
                t_state = None
                d3 = lambda ap: ap.rearrange("p (h i) -> p h i", h=4)
                dsk = bc[:, 2, g * 4:g * 4 + 4].unsqueeze(2).to_broadcast([P, 4, 64])

                def open_chunk(c):
                    sl = slice(c * 128, (c + 1) * 128)
                    bs = BK[3]
                    PE.quiet(lambda e: e.matmul(d3(bs[:, :]), identb[:, :],
                                                maskb[:, :].unsqueeze(1).to_broadcast([P, 4, P]),
                                                start=True, stop=False, skip_group_check=True),
                             t_idb, t_mask, t5, *bs.free)
                    for h in range(4):
                        cc = c * 32 + g * 4 + h
                        tseg = PE.op(lambda e: e.matmul(bs[:, h * 128:(h + 1) * 128],
                                                        AA[:, cc:cc + 1].to_broadcast([P, P]), triu[:, :],
                                                        start=False, stop=(h == 3), skip_group_check=True))
                    bt, bcb = BK[4], BK[5]
                    for j in range(3):
                        tt = PE.op(lambda e: e.transpose(bt[:, j * 128:(j + 1) * 128], F[j][:, sl], ident[:, :]),
                                   ft[j], *bt.free)
                    tcb = PE.op(lambda e: e.matmul(bcb[:, 0:128], F[2][:, sl], F[3][:, sl], start=True, stop=True),
                                ft[2], ft[3], *bcb.free)
                    d = dec.next()
                    for h in range(4):
                        cc = c * 32 + g * 4 + h
                        td = ACT.op(lambda e: e.activation(d[:, h * 128:(h + 1) * 128], bs[:, h * 128:(h + 1) * 128],
                                                           ACTF.Exp, bias=NCU[:, cc:cc + 1]), tseg, t7, *d.free)
                    bs.free = [td]
                    a, b, w, n = xdt.next(), xd.next(), xw.next(), bn.next()
                    t1 = DVE.op(lambda e: e.tensor_tensor(h4(a[:, :]), h4(bt[:, 0:256]), colh(DT, c), ALU.mult),
                                tt, *t_dec, *a.free)
                    t2 = DVE.op(lambda e: e.tensor_tensor(h4(b[:, :]), h4(bt[:, 0:256]), dsk, ALU.mult), tt, t_bc, *b.free)
                    t3 = DVE.op(lambda e: e.tensor_tensor(h4(w[:, :]), h4(a[:, :]), colh(WE, c), ALU.mult), t1, *w.free)
                    t4 = ACT.op(lambda e: e.activation(n[:, :], bt[:, 256:384], ACTF.Copy), tt, t2, *n.free)
                    bt.free = [t4]
                    tM = DVE.op(lambda e: e.tensor_tensor(d3(d[:, :]), d3(d[:, :]),
                                                          bcb[:, 0:128].unsqueeze(1).to_broadcast([P, 4, P]), ALU.mult),
                                td, tcb)
                    bcb.free = [tM]
                    return d, a, b, w, n, t1, t2, t3, t4, tM

                opened = open_chunk(0)
                yield
                for c in range(NC):
                    sl = slice(c * 128, (c + 1) * 128)
                    d, a, b, w, n, t1, t2, t3, t4, tM = opened
                    if c < NC - 1:
                        opened = open_chunk(c + 1)
                        yield
                    by, bz = BK[6], BK[7]
                    for j in range(2):
                        tz = PE.op(lambda e: e.transpose(bz[:, j * 128:(j + 1) * 128], F[4 + j][:, sl], ident[:, :]),
                                   ft[4 + j], *bz.free)
                    if c < NC - 1:
                        tup = PE.op(lambda e: e.matmul(bz[:, 256:512], n[:, :], w[:, :], start=True, stop=True), t3, t4)
                    else:
                        tup = tz
                    for h in range(4):
                        tmm = PE.op(lambda e: e.matmul(by[:, h * 64:(h + 1) * 64], d[:, h * 128:(h + 1) * 128],
                                                       a[:, h * 64:(h + 1) * 64], start=True, stop=True),
                                    tM, t1, *by.free)
                    tin = tmm
                    if c > 0:
                        tin = PE.op(lambda e: e.matmul(by[:, 256:512], F[3][:, sl], state[:, :], start=True, stop=True),
                                    t_state)
                    d.free, a.free, n.free, w.free = [tmm], [tmm, t3], [tup], [tup]
                    if c == 0:
                        t_state = DVE.op(lambda e: e.tensor_copy(state[:, :], bz[:, 256:512]), tup, *state.free)
                    elif c < NC - 1:
                        s2 = DVE.op(lambda e: e.tensor_tensor(h4(state[:, :]), h4(state[:, :]), colh(EL, c), ALU.mult),
                                    tin, t_state)
                        t_state = DVE.op(lambda e: e.tensor_tensor(state[:, :], state[:, :], bz[:, 256:512], ALU.add),
                                         s2, tup)
                    else:
                        state.free = [tin]
                    yc = yv[:, c, :]
                    t6 = DVE.op(lambda e: e.tensor_tensor(yc, by[:, 0:256], b[:, :], ALU.add), tin, t2, *yv.free)
                    by.free = [t6]
                    if c > 0:
                        s1 = DVE.op(lambda e: e.tensor_tensor(h4(b[:, :]), h4(by[:, 256:512]), colh(EC, c), ALU.mult),
                                    tin, t6)
                        by.free = [s1]
                        t6 = DVE.op(lambda e: e.tensor_tensor(yc, yc, b[:, :], ALU.add), s1, t6)
                    t6 = DVE.op(lambda e: e.scalar_tensor_tensor(out=yc, in0=bz[:, 0:256], scalar=0.5, in1=yc,
                                                                 op0=ALU.mult, op1=ALU.mult), t6, tz, tup)
                    bz.free = [t6]
                    tq = DVE.op(lambda e: e.tensor_tensor_reduce(b[:, :], yc, yc, 1.0, 0.0, ALU.mult, ALU.add,
                                                                 small[:, 8 + c:9 + c]), t6)
                    b.free = [tq]
                    yield
                for j in range(6):
                    F[j].free = [tin, tz]
                ts = ACT.op(lambda e: e.activation(small[:, 12:16], small[:, 8:12], ACTF.Sqrt, bias=EPS,
                                                   scale=1.0 / 256), tq)
                ts = DVE.op(lambda e: e.reciprocal(small[:, 12:16], small[:, 12:16]), ts)
                for c in range(NC):
                    ts2 = DVE.op(lambda e, c=c: e.tensor_scalar(yv[:, c, :], yv[:, c, :], small[:, 12 + c:13 + c], None,
                                                               ALU.mult), ts)
                yield
                bz = BK[7]
                for j in range(2):
                    for c in range(NC):
                        tt = PE.op(lambda e, j=j, c=c: e.transpose(bz[:, c * 128:(c + 1) * 128],
                                                                   yv[:, c, j * 128:(j + 1) * 128], ident[:, :]),
                                   ts2, *bz.free)
                    t1 = ACT.op(lambda e, j=j: e.activation(YB[:, 2 * g + j, :], bz[:, :], ACTF.Copy,
                                                           scale=col("ssm_norm_w", 2 * g + j)), tt, t_xdead)
                    bz.free = [t1]
                    ybtok[2 * g + j] = t1
                    yield
                yv.free = [tt]
                ssd_done[:] = [tt, t1, ts2, tin]
                yield

            ybtok = [None] * 16
            ssd_done = []
            side = iter(())

            def steps(n):
                for _ in range(n):
                    if next(side, done) is done:
                        return

            step1 = lambda: steps(1)
            for g in range(8):
                F, ft = cf[g % 2], []
                for j, tile in enumerate((2 * g, 2 * g + 1, 16 + g, 24 + g)):
                    bk, tm = gemm(Hh, Hl, htok, hook=step1, every=2)
                    ft.append(conv(bk, tm, tile, F[j]))
                    t_mm = mods(1, 16 + 4 * g + j)
                for j in range(2):
                    bk, tm = gemm(Hh, Hl, htok, hook=step1, every=2)
                    q = tmp.next()
                    t = ACT.op(lambda e: e.activation(q[:, :], bk[:, :], ACTF.Tanh, scale=0.5), tm, *q.free)
                    t = DVE.op(lambda e: e.scalar_tensor_tensor(out=F[4 + j][:, :], in0=q[:, :], scalar=1.0, in1=bk[:, :],
                                                                op0=ALU.add, op1=ALU.mult), t, *F[4 + j].free)
                    bk.free = q.free = [t]
                    ft.append(t)
                steps(99)
                side = ssd(g, F, ft)
            t_modall = t_mm
            t_op2 = DVE.op(lambda e: e.tensor_scalar(opc[:, 8:16], modc[:, 32:40], 1.0, None, ALU.add), t_modall)

            s_ws = sem("s_ws")
            vt = []
            for m in range(KT):
                bk, tm = gemm(Hh, Hl, htok, hook=step1, every=2)
                b = tmp.next()
                t1 = ACT.op(lambda e, bk=bk, b=b: e.activation(b[:, :], bk[:, :], ACTF.Gelu_apprx_tanh), tm, *b.free)
                bk.free = [t1]
                vt.append((b, t1, m))
                while vt and (len(vt) > 1 or m == KT - 1):
                    b, t1, mm = vt.pop(0)
                    bt = MB.next()
                    for c in range(NC):
                        tt = PE.op(lambda e, c=c, b=b, bt=bt: e.transpose(bt[:, c * 128:(c + 1) * 128],
                                                                  b[:, c * 128:(c + 1) * 128], ident[:, :]),
                                   t1, *bt.free)
                    b.free = [tt]
                    t_v = ACT.op(lambda e, mm=mm, bt=bt: e.activation(V[:, :, mm * 128:(mm + 1) * 128],
                                                              bt[:, :].rearrange("p (c d) -> p c d", c=NC), ACTF.Copy),
                                 tt)
                    bt.free = [t_v]
            steps(99)
            t_ws = SP.dma(lambda e: e.dma_start(wraw[:, :, :], A["gm_ws"][0].rearrange("g i j -> i g j")), s_ws, 16,
                          *ssd_done)
            for q in range(2):
                bk = BK[5 + q]
                for j in range(4):
                    tt = PE.op(lambda e, j=j, q=q, bk=bk: e.transpose(bk[:, j * 128:(j + 1) * 128],
                                                                     wraw[:, 4 * q + j, :], ident[:, :]),
                               t_ws, *bk.free)
                tc = DVE.op(lambda e, q=q, bk=bk: e.tensor_tensor(
                    wsT[:, 4 * q:4 * q + 4, :], bk[:, :].rearrange("p (g i) -> p g i", g=4),
                    triu[:, :].unsqueeze(1).to_broadcast([P, 4, P]), ALU.mult), tt, *ssd_done)
                bk.free = [tc]
            t_wsT = tc
            tv = None
            for c in range(NC):
                vq = wraw[:, :, :].rearrange("p g i -> p (g i)")
                tv = ACT.op(lambda e, c=c: e.activation(vq, V[:, c, :], ACTF.Square,
                                                        accum_out=small[:, 16 + c:17 + c]), t_v, tt, tv)
            ts = ACT.op(lambda e: e.activation(small[:, 16:20], small[:, 16:20], ACTF.Sqrt, bias=EPS, scale=1.0 / D), tv)
            ts = DVE.op(lambda e: e.reciprocal(small[:, 16:20], small[:, 16:20]), ts)
            for c in range(NC):
                tvs = DVE.op(lambda e, c=c: e.tensor_scalar(V[:, c, :], V[:, c, :], small[:, 16 + c:17 + c], None,
                                                           ALU.mult), ts, t_v)
            yatok = [None] * KT

            def sgu(m, u, t_u):
                bk = BK[3 + m % 2]
                for c in range(NC):
                    tt = PE.op(lambda e, c=c: e.matmul(bk[:, c * 128:(c + 1) * 128], V[:, c, m * 128:(m + 1) * 128],
                                                       wsT[:, m, :], start=True, stop=True), tvs, t_wsT, *bk.free)
                q = tmp.next()
                c3 = lambda ap: ap.rearrange("p (c i) -> p c i", c=NC)
                t1 = DVE.op(lambda e: e.scalar_tensor_tensor(
                    out=c3(q[:, :]), in0=c3(bk[:, :]), scalar=col("gm_norm_w", m),
                    in1=bsb[:, m, :].unsqueeze(1).to_broadcast([P, NC, P]), op0=ALU.mult, op1=ALU.add),
                    tt, t_bc, *q.free)
                bk.free = [t1]
                t2 = DVE.op(lambda e: e.tensor_tensor(YA[:, m, :], q[:, :], u[:, :], ALU.mult), t1, t_u)
                q.free = u.free = [t2]
                yatok[m] = t2
                return tt

            last = None
            for m in range(KT):
                bk, tm = gemm(Hh, Hl, htok)
                if last:
                    sgu(*last)
                u = tmp.next()
                t1 = ACT.op(lambda e, bk=bk, u=u: e.activation(u[:, :], bk[:, :], ACTF.Gelu_apprx_tanh), tm, *u.free)
                bk.free = [t1]
                last = (m, u, t1)
            t_vdead = sgu(*last)

            gtok = [[], []]
            for br, (G, gdead) in enumerate(((GA, ssd_done), (GB, [t_vdead]))):
                for m in range(KT):
                    bk, tm = gemm(Hh, Hl, htok)
                    t1 = ACT.op(lambda e, bk=bk, G=G, m=m: e.activation(G[:, m, :], bk[:, :], ACTF.Sigmoid), tm, *gdead)
                    bk.free = [t1]
                    gtok[br].append(t1)
            ya2 = [split(YA[:, m, :], yatok[m], Hh[:, m, :], Hl[:, m, :], [tm]) for m in range(KT)]
            yb2 = [split(YB[:, 8 + m, :], ybtok[8 + m], R2h[:, m, :], R2l[:, m, :], [ya2[-1][0], ya2[-1][1], t_vdead])
                   for m in range(KT)]
            mtok = [None] * KT
            for m in range(KT):
                bk, tm = gemm(Hh, Hl, ya2)
                mtok[m] = DVE.op(lambda e, bk=bk, m=m: e.tensor_tensor(GA[:, m, :], GA[:, m, :], bk[:, :], ALU.mult),
                                 tm, gtok[0][m])
                bk.free = [mtok[m]]
            yb1 = [split(YB[:, m, :], ybtok[m], Hh[:, m, :], Hl[:, m, :], [tm]) for m in range(KT)]
            for X_h, X_l, xt in ((R2h, R2l, yb2), (Hh, Hl, yb1)):
                for m in range(KT):
                    bk, tm = gemm(X_h, X_l, xt)
                    q = tmp.next()
                    t2 = DVE.op(lambda e, bk=bk, q=q, m=m: e.tensor_tensor(q[:, :], GB[:, m, :], bk[:, :], ALU.mult), tm,
                                gtok[1][m], *q.free)
                    bk.free = [t2]
                    mtok[m] = DVE.op(lambda e, q=q, m=m: e.tensor_tensor(GA[:, m, :], GA[:, m, :], q[:, :], ALU.add), t2,
                                     mtok[m])
                    q.free = [mtok[m]]
            t_hdead = tm
            M = GA
            t_ydead = tm
            mm_tok = [split(M[:, m, :], mtok[m], Hh[:, m, :], Hl[:, m, :], [t_hdead]) for m in range(KT)]
            prev = None
            for m in range(KT):
                bk, tm = gemm(Hh, Hl, mm_tok)
                t_hdead = tm
                t1 = DVE.op(lambda e, bk=bk, m=m: e.scalar_tensor_tensor(
                    out=XT[:, m, :], in0=bk[:, :], scalar=modc[:, 16 + m:17 + m], in1=XT[:, m, :],
                    op0=ALU.mult, op1=ALU.add), tm, t_modall, xt_tok[m])
                bk.free = [t1]
                xt_tok[m] = t1
                prev = square_sum(m, XT[:, m, :], t1, prev)
            t_r = rstd_all(prev)
            h2 = [norm_split(m, XT[:, m, :], xt_tok[m], t_r, opc[:, 8 + m:9 + m], modc[:, 24 + m:25 + m], t_op2,
                             [t_hdead]) for m in range(KT)]
            rb.free = [h2[-1][1]]

            fdead = mtok[-1]
            for f in range(2):
                ftok = []
                for m in range(16):
                    bk, tm = gemm(Hh, Hl, h2)
                    t_hdead = tm
                    q = tmp.next()
                    t1 = ACT.op(lambda e, bk=bk, q=q: e.activation(q[:, :], bk[:, :], ACTF.Relu), tm, *q.free)
                    bk.free = [t1]
                    t2 = DVE.op(lambda e, q=q: e.tensor_tensor(q[:, :], q[:, :], q[:, :], ALU.mult), t1)
                    ftok.append(split(q[:, :], t2, YBh[:, m, :], YBl[:, m, :], [fdead]))
                    q.free = [*ftok[-1]]
                prev = None
                for m in range(KT):
                    bk, tm = gemm(YBh, YBl, ftok, 2)
                    fdead = tm
                    t1 = DVE.op(lambda e, bk=bk, m=m: e.scalar_tensor_tensor(
                        out=XT[:, m, :], in0=bk[:, :], scalar=modc[:, 40 + m:41 + m], in1=XT[:, m, :],
                        op0=ALU.mult, op1=ALU.add), tm, t_modall, xt_tok[m])
                    bk.free = [t1]
                    xt_tok[m] = t1
                    if f == 1:
                        prev = square_sum(m, XT[:, m, :], t1, prev)
            t_r = rstd_all(prev)
            for m in range(KT):
                xt_tok[m] = DVE.op(lambda e, m=m: e.scalar_tensor_tensor(
                    out=XT[:, m, :], in0=XT[:, m, :], scalar=col("final_norm_w", m), in1=rb[:, :],
                    op0=ALU.mult, op1=ALU.mult), xt_tok[m], t_r)
            rb.free = [xt_tok[-1]]

        if 2 in blocks:
            if 1 not in blocks:
                t_r = None
            H2 = lambda: None
            names = [("KR0", [P, NC, 2, P]), ("KR1", [P, NC, 2, P]), ("bt0", [P, T]), ("bt1", [P, T]),
                     ("kt0", [P, T]), ("kt1", [P, T]), ("VT", [P, T]), ("Vn", [P, T]), ("KKn", [P, T]), ("Bn", [P, T]),
                     ("Kn", [P, T])]
            for h in range(2):
                names += [(f"{n}{h}", [P, T]) for n in ("Ln", "Xx", "Tt", "AU", "RB", "RK")]
            names += [("Ww0", [P, T]), ("Ww1", [P, T]), ("Qt", [P, T]), ("Gg", [P, T]), ("AV0", [P, 256]), ("AV1", [P, 256]),
                      ("Uu0", [P, P]), ("Uu1", [P, P]), ("Sbd", [P, P]), ("Sf", [P, P])]
            names += [(f"wk{i}", [P, T]) for i in range(5)]
            names += [("Y", [P, KT, T]), ("YT", [P, T]), ("GT", [P, T]), ("BO", [P, T])]
            names += [(f"pad{i}", [P, T + 16]) for i in range(3)]
            names += [("LR", [P, T]), ("WU", [P, T]), ("PW", [P, T]), ("bd", [P, P]), ("fx0", [P, 16]), ("fx1", [P, 16]),
                      ("rc", [P, 16]), ("omka", [P, 4]), ("mt", [P, P])]
            names += [(f"msk{i}", [P, P], mybir.dt.uint8) for i in range(11)]
            Z = {n[0]: t for n, t in zip(names, region(0, *names))}
            B2 = {n: Buf(t) for n, t in Z.items()}
            if 1 not in blocks:
                fdead = tm
            dead = [fdead, *xt_tok]
            s_w2 = sem("s_w2")
            SP.dma(lambda e: e.dma_start(Z["WU"][0:64, :], A["w_up_2"][0]), s_w2, 0, *dead)
            SP.dma(lambda e: e.dma_start(Z["WU"][64:128, :], A["a_up_2"][0]), s_w2, 0)
            SP.dma(lambda e: e.dma_start(Z["PW"][:, :].rearrange("p (g d) -> p g d", g=4),
                                         A["pool_w_2"][0].rearrange("g c d -> c g d")), s_w2, 0)
            t_w2 = (s_w2, 48)

            mt = Z["mt"]
            t_bd = POOL.op(lambda e: e.memset(Z["bd"][:, :], 0.0), *dead)
            t_bd = POOL.op(lambda e: e.memset(Z["bd"][0:64, 0:64], 1.0), t_bd)
            t_bd = POOL.op(lambda e: e.memset(Z["bd"][64:128, 64:128], 1.0), t_bd)
            t_m = t_bd
            LEVELS = [1, 2, 4, 8, 16, 32, 64]
            MX = []
            for q, n in enumerate(LEVELS):
                t_m = POOL.op(lambda e: e.memset(mt[:, :], 0.0), t_m)
                mv = mt[:, :].rearrange("p (b h j) -> p b h j", h=2, j=n)[:, :, 1, :]
                nb = P // (2 * n)
                t_m = POOL.op(lambda e: e.memset(mv, 1.0), t_m)
                t_m = POOL.op(lambda e: e.affine_select(out=mv, in_=mv, compare_op=ALU.is_ge, fill=0.0, base=0,
                                                        pattern=[[-2 * n, nb], [0, n]], channel_multiplier=1), t_m)
                t_m = POOL.op(lambda e: e.affine_select(out=mv, in_=mv, compare_op=ALU.is_ge, fill=0.0, base=n - 1,
                                                        pattern=[[2 * n, nb], [0, n]], channel_multiplier=-1), t_m)
                m8 = Z[f"msk{q}"]
                t_m = POOL.op(lambda e: e.tensor_copy(m8[:, :], mt[:, :]), t_m)
                MX.append(m8)
            t_m = POOL.op(lambda e: e.memset(mt[:, :], 0.0), t_m)
            mv = mt[:, :].rearrange("p (b h) -> p b h", h=2)[:, :, 0]
            t_m = POOL.op(lambda e: e.affine_select(out=mv, in_=mv, compare_op=ALU.not_equal, fill=1.0, base=-1,
                                                    pattern=[[-2, 64]], channel_multiplier=1), t_m)
            t_m = POOL.op(lambda e: e.tensor_copy(Z["msk7"][:, :], mt[:, :]), t_m)
            for q, base, step, mult in ((8, -1, -1, 1), (9, -1, 1, -1), (10, 0, 1, -1)):
                t_m = POOL.op(lambda e: e.affine_select(out=mt[:, :], in_=ones[:, :], compare_op=ALU.is_ge, fill=0.0,
                                                        base=base, pattern=[[step, P]], channel_multiplier=mult), t_m)
                t_m = POOL.op(lambda e: e.tensor_copy(Z[f"msk{q}"][:, :], mt[:, :]), t_m)
            M_LN1, M_LO, M_SU, M_U = (Z[f"msk{q}"] for q in (7, 8, 9, 10))
            t_c0 = None
            for i in range(16):
                t_c0 = DVE.op(lambda e: e.memset(Z["rc"][:, i:i + 1], 1.0 / (i + 1)), *dead)
            for i in range(3):
                t_c0 = DVE.op(lambda e: e.memset(Z[f"pad{i}"][:, 0:16], 0.0))
            for h in range(2):
                for n in ("Ln", "AU", "RB", "RK"):
                    t_c0 = DVE.op(lambda e: e.memset(Z[f"{n}{h}"][:, :], 0.0))
            t_c0 = DVE.op(lambda e: e.memset(Z["Sbd"][:, :], 0.0))
            t_c0 = DVE.op(lambda e: e.tensor_scalar(Z["omka"][:, :], colr("k_a_2", 0, 4), -1.0, 1.0, ALU.mult, ALU.add),
                         t_pc)

            prev = None
            for m in range(KT):
                prev = square_sum(m, XT[:, m, :], xt_tok[m], prev)
            t_r = rstd_all(prev)
            h3 = [norm_split(m, XT[:, m, :], xt_tok[m], t_r, col("norm_gain_2", m), None, t_pc,
                             [] if 1 not in blocks else [t_hdead]) for m in range(KT)]
            rb.free = [h3[-1][1]]
            acc.free = acc.free + [h3[-1][1]]
            wk = Stock([B2[f"wk{i}"] for i in range(5)] + [acc, rb])
            pads = Ring([B2[f"pad{i}"] for i in range(3)])
            c4_ = lambda ap: ap.rearrange("p (c t) -> p c t", c=NC)
            bd = Z["bd"]
            L = EM05

            def shift(bk, tm, tile, dst):
                b, d = pads.next(), tmp.next()
                t1 = ACT.op(lambda e: e.activation(b[:, 16:], bk[:, :], ACTF.Copy), tm, t_c0, *b.free)
                bk.free = [t1]
                t2 = DVE.op(lambda e: e.tensor_tensor(d[:, :], b[:, 15:T + 15], b[:, 16:], ALU.subtract), t1, *d.free)
                t3 = DVE.op(lambda e: e.scalar_tensor_tensor(out=dst[:, :], in0=d[:, :], scalar=col("shift_mu_2", tile),
                                                             in1=b[:, 16:], op0=ALU.mult, op1=ALU.add),
                            t2, t_pc, *dst.free)
                b.free = d.free = [t3]
                return t3

            def head_sums(src, tok):
                bk = MB.next()
                tm = PE.op(lambda e: e.matmul(bk[:, :], bd[:, :], src, start=True, stop=True), tok, t_bd, *bk.free)
                return bk, tm

            bk, tm = gemm(Hh, Hl, h3)
            LR = B2["LR"]
            t_lr = shift(bk, tm, 12, LR)
            t_lr = ACT.op(lambda e: e.activation(LR[0:64, :], LR[0:64, :], ACTF.Tanh), t_lr)

            sets = [dict(KR=B2[f"KR{i}"], bt=B2[f"bt{i}"], kt=B2[f"kt{i}"], fx=B2[f"fx{i}"]) for i in range(2)]
            cur = {}

            def decays(f):
                s = cur[f] = dict(sets[f % 2])
                fx = s["fx"]
                sg, a, cs, ip = (wk.get() for _ in range(4))
                out2 = []
                for q, dst, name in ((0, sg, "w0_2"), (64, a, "a0_2")):
                    bk = MB.next()
                    tm = PE.op(lambda e: e.matmul(bk[:, :], Z["WU"][q:q + 64, f * 128:(f + 1) * 128], LR[q:q + 64, :],
                                                  start=True, stop=True), t_lr, t_w2, *bk.free)
                    t = ACT.op(lambda e: e.activation(dst[:, :], bk[:, :], ACTF.Sigmoid, bias=col(name, f)), tm, t_pc,
                               *dst.free)
                    bk.free = [t]
                    out2.append(t)
                t_sg, s["ta"] = out2
                for c in range(NC):
                    sl = slice(c * 128, (c + 1) * 128)
                    t1 = DVE.op(lambda e: e.tensor_tensor_scan(cs[:, sl], ones[:, :], sg[:, sl], 0.0, ALU.mult, ALU.add),
                                t_sg, t_ones, *cs.free)
                t2 = DVE.op(lambda e: e.tensor_copy(fx[:, 0:4], c4_(cs[:, :])[:, :, 63]), t1, *fx.free)
                t3 = DVE.op(lambda e: e.tensor_tensor(c4_(cs[:, :]), c4_(cs[:, :]),
                                                      fx[:, 0:4].unsqueeze(2).to_broadcast([P, NC, P]), ALU.subtract), t2)
                t4 = DVE.op(lambda e: e.tensor_tensor(sg[:, :], cs[:, :], sg[:, :], ALU.subtract), t3)
                t5 = ACT.op(lambda e: e.activation(fx[:, 4:8], fx[:, 0:4], ACTF.Exp, scale=-L), t2)
                t5 = ACT.op(lambda e: e.activation(fx[:, 8:12], c4_(cs[:, :])[:, :, 127], ACTF.Exp, scale=-L), t3)
                s["tfac"] = DVE.op(lambda e: e.tensor_tensor(fx[:, 12:15], fx[:, 8:11], fx[:, 5:8], ALU.mult), t5)
                s["tip"] = ACT.op(lambda e: e.activation(ip[:, :], cs[:, :], ACTF.Exp, scale=L), t3, *ip.free)
                s["trp"] = ACT.op(lambda e: e.activation(cs[:, :], cs[:, :], ACTF.Exp, scale=-L), t5, t4)
                s["tpp"] = ACT.op(lambda e: e.activation(sg[:, :], sg[:, :], ACTF.Exp, scale=-L), t4)
                s.update(pp=sg, a=a, rp=cs, ip=ip)

            def keys(f, bk, tm):
                s = cur[f]
                k, kk = wk.get(), wk.get()
                tk = shift(bk, tm, 4 + f, k)
                t1 = DVE.op(lambda e: e.tensor_scalar(kk[:, :], k[:, :], col("k_k_2", f), None, ALU.mult), tk, *kk.free)
                q = tmp.next()
                t2 = ACT.op(lambda e: e.activation(q[:, :], kk[:, :], ACTF.Square), t1, *q.free)
                b, tm = head_sums(q[:, :], t2)
                t3 = ACT.op(lambda e: e.activation(q[:, :], b[:, :], ACTF.Sqrt), tm)
                b.free = [t3]
                t3 = DVE.op(lambda e: e.tensor_scalar(q[:, :], q[:, :], 1e-12, None, ALU.max), t3)
                t3 = DVE.op(lambda e: e.reciprocal(q[:, :], q[:, :]), t3)
                t3 = DVE.op(lambda e: e.tensor_tensor(kk[:, :], kk[:, :], q[:, :], ALU.mult), t3, t1)
                t4 = DVE.op(lambda e: e.tensor_scalar(q[:, :], s["a"][:, :], col("k_a_2", f), Z["omka"][:, f:f + 1],
                                                      ALU.mult, ALU.add), s["ta"], t3)
                t4 = DVE.op(lambda e: e.tensor_tensor(k[:, :], k[:, :], q[:, :], ALU.mult), t4)
                q.free = [t4]
                KR = s["KR"]
                t5 = DVE.op(lambda e: e.scalar_tensor_tensor(out=KR[:, :, 0, :], in0=c4_(kk[:, :]), scalar=-1.0,
                                                             in1=c4_(s["pp"][:, :]), op0=ALU.mult, op1=ALU.mult),
                            t3, s["tpp"], *KR.free)
                t6 = DVE.op(lambda e: e.tensor_tensor(kk[:, :], kk[:, :], s["a"][:, :], ALU.mult), t5, s["ta"])
                t6 = DVE.op(lambda e: e.tensor_tensor(s["bt"][:, :], kk[:, :], s["ip"][:, :], ALU.mult), t6, s["tip"],
                            *s["bt"].free)
                t7 = DVE.op(lambda e: e.tensor_tensor(s["kt"][:, :], k[:, :], s["ip"][:, :], ALU.mult), t4,
                            *s["kt"].free)
                s.update(tkk=t5, tb=t6, tkt=t7, k2=k, tk2=t4)
                wk.give(kk, t6)
                wk.give(s["pp"], t5)
                wk.give(s["a"], t6)
                wk.give(s["ip"], t7)

            def receptance(f, bk, tm):
                s = cur[f]
                r = wk.get()
                tr = shift(bk, tm, f, r)
                s["tr"] = DVE.op(lambda e: e.tensor_tensor(s["KR"][:, :, 1, :], c4_(r[:, :]), c4_(s["rp"][:, :]), ALU.mult),
                                 tr, s["trp"], *s["KR"].free)
                t2 = DVE.op(lambda e: e.scalar_tensor_tensor(out=r[:, :], in0=r[:, :], scalar=col("r_k_2", f),
                                                             in1=s["k2"][:, :], op0=ALU.mult, op1=ALU.mult),
                            s["tr"], s["tk2"])
                wk.give(s["rp"], s["tr"])
                wk.give(s["k2"], t2, s["tkt"])
                s.update(rk=r, trk=t2)

            def values(f, bk, tm):
                s = cur[f]
                V2, BO = B2["VT"], B2["BO"]
                s["tv"] = shift(bk, tm, 8 + f, V2)
                b, tm = head_sums(s["rk"][:, :], s["trk"])
                wk.give(s["rk"], tm)
                s["tbo"] = DVE.op(lambda e: e.tensor_tensor(BO[:, :], V2[:, :], b[:, :], ALU.mult), tm, s["tv"], *BO.free)
                b.free = [s["tbo"]]

            R4 = lambda ap: ap.rearrange("p (c t) -> p c t", c=NC)
            m4 = lambda m: m[:, :].unsqueeze(1).to_broadcast([P, NC, P])

            def head(f, hp, res):
                s = cur[f]
                b0, b1 = BK[3 + 2 * hp], BK[4 + 2 * hp]
                rows = slice(64 * hp, 64 * hp + 64)
                Ln, Xx, Tt, AU, RB, RK = (B2[f"{n}{hp}"] for n in ("Ln", "Xx", "Tt", "AU", "RB", "RK"))
                t_tT = t_x0 = None
                tg = {}
                gt = (s["tkk"], s["tb"], s["tkt"], s["tr"])
                ti = ACT.op(lambda e: e.activation(R4(Xx[:, :]), ident[:, :].unsqueeze(1).to_broadcast([P, NC, P]),
                                                   ACTF.Copy), t_id, *Xx.free)
                tj = ACT.op(lambda e: e.activation(R4(Tt[:, :]), ident[:, :].unsqueeze(1).to_broadcast([P, NC, P]),
                                                   ACTF.Copy), t_id, *Tt.free)
                pair = 0
                for left, o0, m0, o1, m1 in (("bt", None, None, RB, M_U), ("kt", AU, M_SU, RK, M_U)):
                    for half in range(2):
                        bk = (b0, b1)[half]
                        for cc in range(2):
                            c = 2 * half + cc
                            tg = PE.op(lambda e: e.matmul(bk[:, cc * 256:(cc + 1) * 256].rearrange("p (a t) -> p a t", a=2),
                                                          s[left][rows, c * 128:(c + 1) * 128], s["KR"][rows, c, :, :],
                                                          start=True, stop=True), *gt, *bk.free)
                        v = bk[:, :].rearrange("p (c a t) -> p c a t", c=2, a=2)
                        hs = slice(2 * half, 2 * half + 2)
                        m2 = lambda m: m[:, :].unsqueeze(1).to_broadcast([P, 2, P])
                        if o0 is None:
                            t1 = DVE.op(lambda e: e.copy_predicated(R4(Xx[:, :])[:, hs, :], m2(MX[0]), v[:, :, 0, :]),
                                        tg, ti, t_m)
                        else:
                            t1 = DVE.op(lambda e: e.copy_predicated(R4(o0[:, :])[:, hs, :], m2(m0), v[:, :, 0, :]),
                                        tg, t_m, t_c0, *o0.free)
                        t2 = DVE.op(lambda e: e.copy_predicated(R4(o1[:, :])[:, hs, :], m2(m1), v[:, :, 1, :]),
                                    tg, t_m, t_c0, *o1.free)
                        bk.free = [t2, t1]
                        if o0 is None:
                            t_x = t1
                            t_rb = t2
                        else:
                            t_au, t_rk = t1, t2
                    yield
                for c in range(NC):
                    tg = PE.op(lambda e: e.matmul(b0[:, c * 128:(c + 1) * 128], s["KR"][rows, c, 0, :],
                                                  s["bt"][rows, c * 128:(c + 1) * 128], start=True, stop=True),
                               *b0.free)
                t1 = DVE.op(lambda e: e.copy_predicated(R4(Tt[:, :]), m4(M_LN1), R4(b0[:, :])), tg, tj, t_m)
                t_ln = DVE.op(lambda e: e.copy_predicated(R4(Ln[:, :]), m4(M_LO), R4(b0[:, :])), tg, t_c0, t_m, *Ln.free)
                b0.free = [t_ln]
                t_t = t1
                yield
                w = B2[f"Ww{hp}"]
                for q in range(1, 7):
                    for c in range(NC):
                        sl = slice(c * 128, (c + 1) * 128)
                        tw = PE.op(lambda e: e.matmul(b0[:, sl], Ln[:, sl], Xx[:, sl], start=True, stop=True),
                                   t_ln, t_x, *b0.free)
                    tw = ACT.op(lambda e: e.activation(w[:, :], b0[:, :], ACTF.Copy), tw, *w.free)
                    b0.free = [tw]
                    yield
                    for c in range(NC):
                        sl = slice(c * 128, (c + 1) * 128)
                        tx = PE.op(lambda e: e.matmul(b1[:, sl], Tt[:, sl], w[:, sl], start=True, stop=True),
                                   tw, t_t, *b1.free)
                    w.free = [tx]
                    t_x = DVE.op(lambda e: e.copy_predicated(R4(Xx[:, :]), m4(MX[q]), R4(b1[:, :])), tx)
                    b1.free = [t_x]
                    yield
                    if q < 6:
                        for c in range(NC):
                            sl = slice(c * 128, (c + 1) * 128)
                            tt = PE.op(lambda e: e.transpose(b1[:, sl], Xx[:, sl], ident[:, :]), t_x, *b1.free)
                        t_t = ACT.op(lambda e: e.activation(Tt[:, :], b1[:, :], ACTF.Copy), tt)
                        b1.free = [t_t]
                res.update({("x", hp): t_x, ("au", hp): t_au, ("rb", hp): t_rb, ("rk", hp): t_rk})
                Ln.free = [tw]
                Tt.free = [tx]

            def rwkv(f):
                s = cur[f]
                KR = s["KR"]
                Vn, KKn, Bn, Kn, YT, GT, BO = (B2[n] for n in ("Vn", "KKn", "Bn", "Kn", "YT", "GT", "BO"))
                Qt, G, Sbd, Sf = (B2[n] for n in ("Qt", "Gg", "Sbd", "Sf"))
                bs = BK[7]
                nat = {}
                for n, dst, src, tok in (("v", Vn, lambda c: B2["VT"][:, c * 128:(c + 1) * 128], s["tv"]),
                                         ("kk", KKn, lambda c: KR[:, c, 0, :], s["tkk"]),
                                         ("b", Bn, lambda c: s["bt"][:, c * 128:(c + 1) * 128], s["tb"]),
                                         ("k", Kn, lambda c: s["kt"][:, c * 128:(c + 1) * 128], s["tkt"])):
                    for c in range(NC):
                        tt = PE.op(lambda e: e.transpose(bs[:, c * 128:(c + 1) * 128], src(c), ident[:, :]), tok, *bs.free)
                    if n == "v":
                        B2["VT"].free = [tt, s["tbo"]]
                    nat[n] = ACT.op(lambda e: e.activation(dst[:, :], bs[:, :], ACTF.Copy), tt, *dst.free)
                    bs.free = [nat[n]]
                    yield
                res = {}
                gens = [head(f, 0, res), head(f, 1, res)]
                while gens:
                    for g in list(gens):
                        if next(g, done) is done:
                            gens.remove(g)
                        yield
                av, tg = [B2["AV0"], B2["AV1"]], []
                for hp in range(2):
                    b0 = BK[3 + 2 * hp]
                    for c in range(NC):
                        tm = PE.op(lambda e: e.matmul(b0[:, c * 64:(c + 1) * 64], B2[f"AU{hp}"][:, c * 128:(c + 1) * 128],
                                                      Vn[:, c * 128 + 64 * hp:c * 128 + 64 * hp + 64],
                                                      start=True, stop=True), res[("au", hp)], nat["v"], *b0.free)
                    t = DVE.op(lambda e: e.tensor_copy(av[hp][:, :], b0[:, 0:256]), tm, *av[hp].free)
                    b0.free = [t]
                    tg.append(t)
                    B2[f"AU{hp}"].free = [tm]
                yield
                b1 = BK[4]
                for hp in range(2):
                    for c in range(NC):
                        tq = PE.op(lambda e: e.matmul(b1[64 * hp:64 * hp + 64, c * 128:(c + 1) * 128],
                                                      KKn[:, c * 128 + 64 * hp:c * 128 + 64 * hp + 64],
                                                      B2[f"Xx{hp}"][:, c * 128:(c + 1) * 128], start=True, stop=True),
                                   res[("x", hp)], nat["kk"], *b1.free)
                t_q = ACT.op(lambda e: e.activation(Qt[:, :], b1[:, :], ACTF.Copy), tq, *Qt.free)
                b1.free = [t_q]
                KKn.free = [tq]
                b1 = BK[6]
                for hp in range(2):
                    for c in range(NC):
                        tq = PE.op(lambda e: e.matmul(b1[:, c * 128 + 64 * hp:c * 128 + 64 * hp + 64],
                                                      B2[f"Xx{hp}"][:, c * 128:(c + 1) * 128],
                                                      av[hp][:, c * 64:(c + 1) * 64], start=True, stop=True),
                                   tg[hp], *b1.free)
                    av[hp].free = [tq]
                    B2[f"Xx{hp}"].free = [tq]
                t_g = ACT.op(lambda e: e.activation(G[:, :], b1[:, :], ACTF.Copy), tq, *G.free)
                b1.free = [t_g]
                yield
                t_s = None
                for c in range(NC):
                    sl = slice(c * 128, (c + 1) * 128)
                    by, bu = BK[3], BK[5]
                    if c == 0:
                        U, t_u, uof = G, t_g, 0
                        Ua = G[:, 0:128]
                    else:
                        Ub = B2[f"Uu{c % 2}"]
                        Ua = Ub[:, :]
                        tm = PE.op(lambda e: e.matmul(bu[:, 0:128], Qt[:, sl], Sbd[:, :], start=True, stop=True),
                                   t_q, t_s, *bu.free)
                        t_u = DVE.op(lambda e: e.tensor_tensor(Ua, bu[:, 0:128], G[:, sl], ALU.add), tm, t_g, *Ub.free)
                        bu.free = [t_u]
                        tf = None
                        if c < NC - 1:
                            tf = DVE.op(lambda e: e.tensor_scalar(Sf[:, :], Sbd[:, :], s["fx"][:, 12 + c:13 + c], None,
                                                                  ALU.mult), t_s, s["tfac"])
                        yield
                    if c < NC - 1:
                        bq = BK[4]
                        tm = PE.op(lambda e: e.matmul(bq[:, 0:128], Kn[:, sl], Vn[:, sl], start=True, stop=False),
                                   nat["k"], nat["v"], *bq.free)
                        tm = PE.op(lambda e: e.matmul(bq[:, 0:128], Bn[:, sl], Ua, start=False, stop=True), nat["b"], t_u)
                    if c > 0:
                        ty = PE.op(lambda e: e.matmul(by[:, 0:128], Sbd[:, :], KR[:, c, 1, :], start=True, stop=False,
                                                      skip_group_check=True), t_s, *by.free)
                    for hp in range(2):
                        vs = slice(64 * hp, 64 * hp + 64)
                        ty = PE.op(lambda e: e.matmul(by[vs, 0:128], Vn[:, c * 128 + 64 * hp:c * 128 + 64 * hp + 64],
                                                      B2[f"RK{hp}"][:, sl], start=(c == 0), stop=False,
                                                      skip_group_check=True), res[("rk", hp)], nat["v"], *by.free)
                        ty = PE.op(lambda e: e.matmul(by[vs, 0:128], Ua[:, vs], B2[f"RB{hp}"][:, sl], start=False,
                                                      stop=True, skip_group_check=True), res[("rb", hp)], t_u)
                    if c > 0:
                        Ub.free = [ty]
                    if c < NC - 1:
                        for hp in range(2):
                            vs = slice(64 * hp, 64 * hp + 64)
                            if c == 0:
                                t = DVE.op(lambda e: e.tensor_scalar(Sbd[vs, vs], bq[vs, vs], s["fx"][vs, 12:13], None,
                                                                     ALU.mult), tm, s["tfac"], t_c0, *Sbd.free)
                            else:
                                t = DVE.op(lambda e: e.scalar_tensor_tensor(
                                    out=Sbd[vs, vs], in0=bq[vs, vs], scalar=s["fx"][vs, 12 + c:13 + c], in1=Sf[vs, vs],
                                    op0=ALU.mult, op1=ALU.add), tm, tf, ty)
                        t_s = t
                        bq.free = [t]
                    t_y = ACT.op(lambda e: e.activation(YT[:, sl], by[:, 0:128], ACTF.Copy), ty, *YT.free)
                    by.free = [t_y]
                    yield
                Sbd.free = [ty]
                for n in ("Vn", "Kn", "Bn", "Qt"):
                    B2[n].free = [ty]
                G.free = [ty, t_u]
                for hp in range(2):
                    B2[f"RB{hp}"].free = B2[f"RK{hp}"].free = [ty]
                KR.free = s["bt"].free = s["kt"].free = [ty]
                s["fx"].free = [t_s]
                b = bs
                tm = PE.op(lambda e: e.matmul(b[:, :], bd[:, :], YT[:, :], start=True, stop=True), t_y, *b.free)
                t1 = DVE.op(lambda e: e.scalar_tensor_tensor(out=YT[:, :], in0=b[:, :], scalar=-1.0 / 64, in1=YT[:, :],
                                                             op0=ALU.mult, op1=ALU.add), tm, t_y)
                b.free = [t1]
                q = wk2.next()
                t2 = ACT.op(lambda e: e.activation(q[:, :], YT[:, :], ACTF.Square), t1, *q.free)
                yield
                tm = PE.op(lambda e: e.matmul(b[:, :], bd[:, :], q[:, :], start=True, stop=True), t2, *b.free)
                t3 = ACT.op(lambda e: e.activation(q[:, :], b[:, :], ACTF.Sqrt, bias=GEPS, scale=1.0 / 64), tm)
                b.free = [t3]
                yield
                t3 = DVE.op(lambda e: e.reciprocal(q[:, :], q[:, :]), t3)
                t4 = DVE.op(lambda e: e.scalar_tensor_tensor(out=YT[:, :], in0=YT[:, :], scalar=col("gn_gain_2", f),
                                                             in1=q[:, :], op0=ALU.mult, op1=ALU.mult), t3, t1)
                q.free = [t4]
                t5 = DVE.op(lambda e: e.scalar_tensor_tensor(out=YT[:, :], in0=YT[:, :], scalar=col("gn_bias_2", f),
                                                             in1=BO[:, :], op0=ALU.add, op1=ALU.add), t4, s["tbo"])
                BO.free = [t5]
                while f not in gate:
                    yield
                t6 = DVE.op(lambda e: e.tensor_tensor(Y[:, 4 + f, :], YT[:, :], GT[:, :], ALU.mult), t5, gate[f])
                YT.free = GT.free = [t6]
                yt2[4 + f] = t6
                yield

            Y = Z["Y"]
            yt2 = [None] * KT
            gate = {}
            wk2 = Ring([B2["Ww0"], B2["Ww1"]])
            t_hd = None
            pooled = {}

            def pool_u(m, bk, tm):
                b = pads.next()
                t1 = ACT.op(lambda e: e.activation(b[:, 16:], bk[:, :], ACTF.Copy), tm, *b.free)
                bk.free = [t1]
                src, n = b, 1
                others = [pads.next(), pads.next()]
                while n < 2 << m:
                    dst = others[0]
                    others.reverse()
                    t1 = DVE.op(lambda e: e.tensor_tensor(dst[:, 16:], src[:, 16:], src[:, 16 - n:T + 16 - n], ALU.add),
                                t1, *dst.free)
                    src, n = dst, 2 * n
                q = wk.get()
                t2 = DVE.op(lambda e: e.scalar_tensor_tensor(out=q[:, :], in0=src[:, 16:], scalar=1.0 / n, in1=b[:, 16:],
                                                             op0=ALU.mult, op1=ALU.subtract), t1, *q.free)
                t3 = DVE.op(lambda e: e.tensor_tensor(q[:, 0:n - 1], src[:, 16:16 + n - 1], Z["rc"][:, 0:n - 1], ALU.mult),
                            t2)
                t3 = DVE.op(lambda e: e.tensor_tensor(q[:, 0:n - 1], q[:, 0:n - 1], b[:, 16:16 + n - 1], ALU.subtract), t3)
                for x in (b, *others):
                    x.free = [t3]
                pooled[m] = (q, t3)

            def pool_g(m, bk, tm):
                q, tq = pooled[m]
                g = tmp.next()
                t1 = ACT.op(lambda e: e.activation(g[:, :], bk[:, :], ACTF.Silu), tm, *g.free)
                bk.free = [t1]
                b = MB.next()
                tmm = PE.op(lambda e: e.matmul(b[:, :], Z["PW"][:, m * 128:(m + 1) * 128], q[:, :], start=True, stop=True),
                            tq, t_w2, *b.free)
                wk.give(q, tmm)
                yt2[m] = DVE.op(lambda e: e.scalar_tensor_tensor(out=Y[:, m, :], in0=b[:, :], scalar=col("pool_scale_2", m),
                                                                 in1=g[:, :], op0=ALU.mult, op1=ALU.mult), tmm, t1)
                b.free = g.free = [yt2[m]]

            def gate_b(m, bk, tm):
                t = ACT.op(lambda e: e.activation(B2["GT"][:, :], bk[:, :], ACTF.Silu), tm, *B2["GT"].free)
                bk.free = [t]
                gate[m] = t

            side2 = [iter(())]

            def step2():
                next(side2[0], done)

            decays(0)
            for n, m in ORDER2:
                bk, tm = gemm(Hh, Hl, h3, hook=step2)
                t_hd = tm
                if n == "k":
                    keys(m, bk, tm)
                elif n == "r":
                    receptance(m, bk, tm)
                elif n == "v":
                    if m > 0:
                        for _ in side2[0]:
                            pass
                    values(m, bk, tm)
                    side2[0] = rwkv(m)
                    if m < 3:
                        decays(m + 1)
                elif n == "ua":
                    pool_u(m, bk, tm)
                elif n == "ga":
                    pool_g(m, bk, tm)
                else:
                    gate_b(m, bk, tm)
            y2 = [split(Y[:, m, :], yt2[m], Hh[:, m, :], Hl[:, m, :], [t_hd]) for m in range(KT - 1)]
            for m in range(KT):
                bk, tm = gemm(Hh, Hl, y2, hook=step2, kt=7)
                xt_tok[m] = DVE.op(lambda e: e.tensor_tensor(XT[:, m, :], XT[:, m, :], bk[:, :], ALU.add), tm, xt_tok[m])
                bk.free = [xt_tok[m]]
            for _ in side2[0]:
                pass
            y2.append(split(Y[:, 7, :], yt2[7], Hh[:, 7, :], Hl[:, 7, :], [t_hd]))
            prev = None
            acc.free = acc.free + [yt2[7]]
            i, sl_ = take("w")
            for m in range(KT):
                bk = MB.next()
                PE.wait(*ready[i], *y2[7], *bk.free)
                for w, x in ((whi, Hh), (whi, Hl), (wlo, Hh)):
                    tm = PE.op(lambda e: e.matmul(bk[:, :], w[sl_][:, m, :], x[:, 7, :], start=(w is whi and x is Hh),
                                                  stop=(w is wlo)))
                t1 = DVE.op(lambda e: e.tensor_tensor(XT[:, m, :], XT[:, m, :], bk[:, :], ALU.add), tm, xt_tok[m])
                bk.free = [t1]
                prev = square_sum(m, XT[:, m, :], t1, prev)
                xt_tok[m] = ACT.op(lambda e: e.activation(XT[:, m, :], XT[:, m, :], ACTF.Copy,
                                                          scale=col("final_gain_2", m)), t1, prev)
            release(i, tm)
            bk = MB.next()
            for c in range(NC):
                tm = PE.op(lambda e: e.matmul(bk[:, c:c + 1], acc[:, c * 128:(c + 1) * 128], ones[:, 0:1],
                                              start=True, stop=True), prev, *bk.free)
            t_os = ACT.op(lambda e: e.activation(small[:, 24:28], bk[:, 0:4], ACTF.Sqrt, bias=EPS, scale=1.0 / D), tm)
            t_os = DVE.op(lambda e: e.reciprocal(small[:, 24:28], small[:, 24:28]), t_os)
            odead = [y2[-1][0], y2[-1][1], yt2[7]]
        else:
            t_os = DVE.op(lambda e: e.memset(small[:, 24:28], 1.0))
            odead = []

        OT, = region(0, ("OT", [P, 2, D]))
        ofree = [None, None]
        for c in range(NC):
            for q in range(2):
                bk = BK[3 + (2 * c + q) % 4]
                for j in range(4):
                    m = q * 4 + j
                    tt = PE.op(lambda e, m=m, j=j, c=c, bk=bk: e.transpose(bk[:, j * 128:(j + 1) * 128],
                                                                          XT[:, m, c * 128:(c + 1) * 128], ident[:, :]),
                               xt_tok[m], *bk.free)
                to = ACT.op(lambda e, c=c, q=q, bk=bk: e.activation(OT[:, c % 2, q * 512:(q + 1) * 512], bk[:, :],
                                                                   ACTF.Copy, scale=small[:, 24 + c:25 + c]),
                            tt, t_os, ofree[c % 2], *odead)
                bk.free = [to]
            ofree[c % 2] = SP.dma(lambda e, c=c: e.dma_start(out[0, c * 128:(c + 1) * 128, :], OT[:, c % 2, :]),
                                  s_fin[c % 2], 16 * (c // 2 + 1), to)
        SP.wait((s_fin[0], 32), (s_fin[1], 32))


_INS = [
    "x", "c", "w_mod", "b_mod", "w_in", "gm_norm_w", "gm_ws", "gm_bs", "conv_w", "conv_b", "dt_bias", "a_log", "d_skip",
    "ssm_norm_w", "w_branch_gm", "w_branch_ssm", "w_out", "w_ff1", "w_ff2", "final_norm_w", "norm_gain_2",
    "w_in_2", "pool_w_2", "pool_scale_2", "shift_mu_2", "w0_2", "w_up_2", "a0_2", "a_up_2", "k_k_2", "k_a_2", "r_k_2",
    "gn_gain_2", "gn_bias_2", "w_out_2", "final_gain_2",
]
_OUTS = [((1, 512, 1024), "float32")]


def kernel(**inputs):
    import numpy as _np
    import concourse.bacc as _bacc
    from concourse import mybir as _mybir
    from concourse.bass_utils import run_bass_kernel_spmd as _run

    nc = _bacc.Bacc("TRN2", target_bir_lowering=False, num_devices=1)
    arrays, args = {}, {}
    for name in _INS:
        a = _np.ascontiguousarray(inputs[name])
        arrays[f"in_{name}_dram"] = a
        args[name] = nc.dram_tensor(f"in_{name}_dram", a.shape, _mybir.dt.from_np(a.dtype), kind="ExternalInput").ap()
    outs = []
    for i, (shape, dtype) in enumerate(_OUTS):
        dt = _mybir.dt.from_np(_np.dtype(dtype))
        outs.append(nc.dram_tensor(f"out_{i}_dram", shape, dt, kind="ExternalOutput").ap())
    build_program(nc, args, outs[0], BLOCKS)
    r = _run(nc, [arrays], core_ids=[0])
    return r.results[0]["out_0_dram"]
```

```python
from contextlib import ExitStack

import concourse.bass as bass
from concourse import mybir

F32 = mybir.dt.float32
F32R = mybir.dt.float32r
BF16 = mybir.dt.bfloat16
U32 = mybir.dt.uint32
ALU = mybir.AluOpType
ACTF = mybir.ActivationFunctionType
AX_X = mybir.AxisListType.X

P = 128
EM05 = 0.6065306597126334
T = 512
NC = 4
D = 1024
KT = 8
NRAW = 3
NHL = 3
NEG = -1.0e30
BLOCKS = (1, 2)
ORDER2 = [("k", 0), ("r", 0), ("v", 0),
          ("k", 1), ("r", 1), ("gb", 0), ("ua", 0), ("ga", 0), ("v", 1),
          ("k", 2), ("r", 2), ("gb", 1), ("ua", 1), ("ga", 1), ("v", 2),
          ("k", 3), ("r", 3), ("gb", 2), ("ua", 2), ("ga", 2), ("v", 3),
          ("gb", 3), ("ua", 3), ("ga", 3)]




class Queue:

    def __init__(self, eng, sem):
        self.eng, self.sem, self.n, self.seen = eng, sem, 0, {}

    def wait(self, *tokens):
        for t in tokens:
            if t is not None and self.seen.get(id(t[0]), 0) < t[1]:
                self.seen[id(t[0])] = t[1]
                self.eng.wait_ge(t[0], t[1])

    def op(self, fn, *tokens):
        self.wait(*tokens)
        self.n += 1
        fn(self.eng).then_inc(self.sem, 1)
        return (self.sem, self.n)

    def quiet(self, fn, *tokens):
        self.wait(*tokens)
        fn(self.eng)

    def dma(self, fn, sem, value, *tokens):
        self.wait(*tokens)
        fn(self.eng).then_inc(sem, 16)
        return (sem, value)


class Buf:

    def __init__(self, t):
        self.t, self.free, self.sem, self.uses = t, [], None, 0

    def __getitem__(self, k):
        return self.t[k]


class Stock:

    def __init__(self, bufs):
        self.bufs = list(bufs)

    def get(self):
        return self.bufs.pop(0)

    def give(self, b, *tokens):
        b.free = list(tokens)
        self.bufs.append(b)


class Ring:
    def __init__(self, bufs):
        self.bufs, self.i = bufs, 0

    def next(self):
        b = self.bufs[self.i % len(self.bufs)]
        self.i += 1
        return b


def build_program(nc, A, out, blocks=(1, 2)):
    ctx = ExitStack()
    with ctx:
        def sb(name, shape, dt=F32, c=ctx):
            return c.enter_context(nc.sbuf_tensor(name, shape, dt))

        def sem(name):
            return ctx.enter_context(nc.semaphore(name))

        PE, ACT, DVE, POOL, SP = (
            Queue(e, sem(f"s_{n}")) for n, e in (("pe", nc.tensor), ("act", nc.scalar), ("dve", nc.vector),
                                                 ("pool", nc.gpsimd), ("sp", nc.sync)))

        XT = sb("XT", [P, KT, T])
        ident = sb("ident", [P, P])
        ones = sb("ones", [P, P])
        triu = sb("triu", [P, P])
        identb = sb("identb", [P, P], BF16)
        maskb = sb("maskb", [P, P], BF16)
        pcA = sb("pcA", [P, 128])
        pcB = sb("pcB", [P, 128])
        pcC = sb("pcC", [P, 64])
        modc = sb("modc", [P, 48])
        opc = sb("opc", [P, 16])
        small = sb("small", [P, 64])
        cact = sb("cact", [P, 8])
        raw = [Buf(sb(f"raw{i}", [P, KT, 128])) for i in range(NRAW)]
        for i, b in enumerate(raw):
            b.sem = sem(f"s_raw{i}")
        whi = [sb(f"whi{i}", [P, KT, 128], F32R) for i in range(NHL)]
        wlo = [sb(f"wlo{i}", [P, KT, 128], F32R) for i in range(NHL)]
        wfree = [[] for _ in range(NHL)]
        Hh = sb("Hh", [P, KT, T], F32R)
        Hl = sb("Hl", [P, KT, T], F32R)
        tmp = Ring([Buf(sb(f"tmp{i}", [P, T])) for i in range(3)])
        acc = Buf(sb("acc", [P, T]))
        rb = Buf(sb("rb", [P, T]))

        def region(kb, *tensors):
            with ExitStack() as c:
                if kb:
                    sb(f"pad_{tensors[0][0]}", [P, kb * 256], F32, c)
                return [sb(*t, c=c) for t in tensors]

        BK = [Buf(ctx.enter_context(nc.psum_tensor(f"bk{i}", [P, T], F32))) for i in range(8)]
        MB = Ring(BK[0:3])

        plan = []

        def cols(w, c0, n=128, k0=0, kt=KT):
            return w[k0 * 128:(k0 + kt) * 128, c0:c0 + n].rearrange("(k p) n -> p k n", p=P)

        W_IN, W_MOD = A["w_in"][0], A["w_mod"][0]
        OFF = dict(u=0, v=1024, z=2048, x=4096, b=6144, c=7168, dt=8192, ga=8224, gb=9248)

        def add(kind, ap, n=128):
            plan.append((kind, ap, n))

        if 1 in blocks:
            add("w", cols(W_IN, OFF["dt"]))
            for g in range(8):
                for m, c0 in enumerate((OFF["x"] + g * 256, OFF["x"] + g * 256 + 128, OFF["b"] + g * 128,
                                        OFF["c"] + g * 128)):
                    add("w", cols(W_IN, c0))
                    add("mod", cols(W_MOD, (16 + 4 * g + m) * 128))
                for c0 in (OFF["z"] + g * 256, OFF["z"] + g * 256 + 128):
                    add("w", cols(W_IN, c0))
            for m in range(8):
                add("w", cols(W_IN, OFF["v"] + m * 128))
            for m in range(8):
                add("w", cols(W_IN, OFF["u"] + m * 128))
            for m in range(8):
                add("w", cols(W_IN, OFF["ga"] + m * 128))
            for m in range(8):
                add("w", cols(W_IN, OFF["gb"] + m * 128))
            for m in range(8):
                add("w", cols(A["w_branch_gm"][0], m * 128))
            for m in range(8):
                add("w", cols(A["w_branch_ssm"][0], m * 128, k0=8))
            for m in range(8):
                add("w", cols(A["w_branch_ssm"][0], m * 128))
            for m in range(8):
                add("w", cols(A["w_out"][0], m * 128))
            for f in range(2):
                for m in range(16):
                    add("w", cols(A["w_ff1"][0], (f * 16 + m) * 128))
                for m in range(8):
                    add("w", cols(A["w_ff2"][0], m * 128, k0=16 * f))
                    add("w", cols(A["w_ff2"][0], m * 128, k0=16 * f + 8))
        W2 = A["w_in_2"][0]
        OFF2 = dict(ua=0, ga=512, r=1024, k=1536, v=2048, lr=2560, gb=2688)
        if 2 in blocks:
            add("w", cols(W2, OFF2["lr"]))
            for n, m in ORDER2:
                add("w", cols(W2, OFF2[n] + m * 128))
            for m in range(8):
                add("w", cols(A["w_out_2"][0], m * 128, kt=7))
            add("w", A["w_out_2"][0][7 * 128:8 * 128, :].rearrange("p (m n) -> p m n", n=P))

        st = dict(load=0, prep=0, use=0, hl=0)
        ready, slots = {}, {}

        def load():
            i = st["load"]
            st["load"] += 1
            kind, ap, n = plan[i]
            b = raw[i % NRAW]
            kt = ap.shape[1]
            SP.dma(lambda e, b=b, ap=ap, n=n: e.dma_start(b.t[:, 0:kt, 0:n], ap), b.sem, 16 * (i // NRAW + 1), *b.free)

        def prep():
            i = st["prep"]
            st["prep"] += 1
            kind, ap, n = plan[i]
            b = raw[i % NRAW]
            landed = (b.sem, 16 * (i // NRAW + 1))
            if kind == "mod":
                ready[i] = landed
                return
            s = st["hl"] % NHL
            st["hl"] += 1
            slots[i] = s
            kt = ap.shape[1]
            th = ACT.op(lambda e: e.activation(whi[s][:, 0:kt, 0:n], b.t[:, 0:kt, 0:n], ACTF.Copy), landed, *wfree[s])
            tl = DVE.op(lambda e: e.tensor_tensor(wlo[s][:, 0:kt, 0:n], b.t[:, 0:kt, 0:n],
                                                  whi[s][:, 0:kt, 0:n].bitcast(F32), ALU.subtract),
                        landed, th, *wfree[s])
            ready[i] = (th, tl)
            b.free = [tl]

        def take(kind):
            i = st["use"]
            st["use"] += 1
            assert plan[i][0] == kind
            ahead = i + 1
            while True:
                while st["prep"] <= i:
                    while st["load"] <= st["prep"]:
                        load()
                    prep()
                if st["prep"] < len(plan) and st["prep"] <= i + 2:
                    nxt = st["prep"]
                    while st["load"] <= nxt:
                        load()
                    prep()
                    continue
                break
            while st["load"] < len(plan):
                before = st["load"] - NRAW
                if before >= (i if plan[before][0] == "mod" else st["prep"]):
                    break
                load()
            return i, slots.get(i)

        def release(i, tok):
            if plan[i][0] == "mod":
                raw[i % NRAW].free = [tok]
            else:
                wfree[slots[i]] = [tok]

        def gemm(X_h, X_l, xtok, nchunk=1, hook=None, every=1, kt=KT):
            bk = MB.next()
            PE.wait(*bk.free)
            for c in range(nchunk):
                i, s = take("w")
                PE.wait(*ready[i])
                for k in range(kt):
                    kk = c * KT + k
                    PE.wait(*xtok[kk])
                    for w, x in ((whi, X_h), (whi, X_l), (wlo, X_h)):
                        first = kk == 0 and w is whi and x is X_h
                        last = kk == (nchunk - 1) * KT + kt - 1 and w is wlo
                        fn = lambda e, w=w, x=x, k=k, kk=kk, first=first, last=last, s=s: e.matmul(
                            bk.t[:, :], w[s][:, k, :], x[:, kk, :], start=first, stop=last)
                        if k == kt - 1 and w is wlo:
                            tok = PE.op(fn)
                        else:
                            PE.quiet(fn)
                    if hook and (k % 3 == 1 if every == 3 else k % every == every - 1):
                        hook()
                release(i, tok)
            return bk, tok

        tz = POOL.op(lambda e: e.memset(ident[:, :], 0.0))
        t_id = POOL.op(lambda e: e.affine_select(out=ident[:, :], in_=ident[:, :], compare_op=ALU.not_equal, fill=1.0,
                                                 base=0, pattern=[[-1, P]], channel_multiplier=1), tz)
        t_ones = POOL.op(lambda e: e.memset(ones[:, :], 1.0))
        t_triu = POOL.op(lambda e: e.affine_select(out=triu[:, :], in_=ones[:, :], compare_op=ALU.is_ge, fill=0.0,
                                                   base=0, pattern=[[1, P]], channel_multiplier=-1), t_ones)
        t_idb = POOL.op(lambda e: e.tensor_copy(identb[:, :], ident[:, :]), t_id)
        tz = POOL.op(lambda e: e.memset(maskb[:, :], 0.0))
        t_mask = POOL.op(lambda e: e.affine_select(out=maskb[:, :], in_=maskb[:, :], compare_op=ALU.is_ge, fill=NEG,
                                                   base=0, pattern=[[1, P]], channel_multiplier=-1), tz)

        s_par = sem("s_par")
        s_fin = [sem("s_out0"), sem("s_out1")]
        par = {}

        v = lambda name: A[name].rearrange("a (n p) -> (a n) p", p=P)
        v1 = lambda name: A[name].rearrange("(n p) -> n p", p=P)
        rows, where = [], {}

        pr = region(64, *((f"pr{i}", [P, P]) for i in range(3)))

        def put(tile, r, name, ap, n):
            SP.dma(lambda e: e.dma_start(pr[tile][r:r + n, :], ap), s_par, 0)
            where[name] = (tile, r)
            return r + n

        s_x = sem("s_x")
        xnat, xs = region(0, ("xnat", [P, NC, D]), ("xs", [P, NC, D]))
        r = 0
        for name, ap, n in (("c", v("c"), 8), ("b_mod", v("b_mod"), 48), ("conv_b", v("conv_b"), 32),
                            ("gm_norm_w", v("gm_norm_w"), 8), ("ssm_norm_w", v("ssm_norm_w"), 16),
                            ("final_norm_w", v1("final_norm_w"), 8), ("norm_gain_2", v("norm_gain_2"), 8)):
            r = put(1, r, name, ap, n)
        t_par = (s_par, 16 * 7)
        for c in range(NC):
            SP.dma(lambda e, c=c: e.dma_start(xnat[:, c, :], A["x"][0, c * 128:(c + 1) * 128, :]), s_x, 0)
        t_x = (s_x, 64)
        if 1 in blocks:
            wm = region(32, *((f"wm{i}", [P, KT, 256]) for i in range(4)))
            wm += region(73, *((f"wm{i}", [P, KT, 256]) for i in range(4, 8)))
            s_wm = [sem(f"s_wm{i}") for i in range(8)]
            for i in range(8):
                SP.dma(lambda e, i=i: e.dma_start(wm[i][:, :, :], cols(W_MOD, i * 256, 256)), s_wm[i], 16)
        for i in range(3):
            load()
        s_par2 = sem("s_par2")
        s_par, s_par0 = s_par2, s_par
        put(0, 0, "conv_w", A["conv_w"].rearrange("a k (n p) -> (a k n) p", p=P), 128)
        r = 0
        for name, ap, n in (("pool_scale_2", v("pool_scale_2"), 4), ("shift_mu_2", v("shift_mu_2"), 13),
                            ("w0_2", v("w0_2"), 4), ("a0_2", v("a0_2"), 4), ("k_k_2", v("k_k_2"), 4),
                            ("k_a_2", v("k_a_2"), 4),
                            ("r_k_2", A["r_k_2"].rearrange("a (n q) d -> (a n) (q d)", q=2), 4),
                            ("gn_gain_2", v("gn_gain_2"), 4), ("gn_bias_2", v("gn_bias_2"), 4),
                            ("final_gain_2", v1("final_gain_2"), 8)):
            r = put(2, r, name, ap, n)
        rC = r
        tp = []

        def turn(i, dst, n, tok, scale=1.0):
            tm = PE.op(lambda e: e.transpose(BK[i].t[:, 0:n], pr[i][0:n, :], ident[0:n, 0:n]), tok, t_id)
            tp.append(DVE.op(lambda e: e.tensor_scalar(dst[:, 0:n], BK[i].t[:, 0:n], scale, None, ALU.mult), tm))
            BK[i].free = [tp[-1]]

        turn(1, pcB, 128, t_par)
        t_pb = tp[0]
        cw = lambda tap, tile: pcA[:, tap * 32 + tile:tap * 32 + tile + 1]

        def col(name, m):
            tile, r0 = where[name]
            return (pcA, pcB, pcC)[tile][:, r0 + m:r0 + m + 1]

        def colr(name, m, n):
            tile, r0 = where[name]
            return (pcA, pcB, pcC)[tile][:, r0 + m:r0 + m + n]

        t_eps = DVE.op(lambda e: e.memset(small[:, 0:1], 1e-6))
        t_eps = DVE.op(lambda e: e.memset(small[:, 1:2], 64e-5))
        EPS, GEPS = small[:, 0:1], small[:, 1:2]


        warm = small[:, 60:61]

        class Rows:

            def __init__(self, n):
                self.to, self.tok = (acc, rb)[:n], [None, None]

            def add(self, m, tok):
                for i, to in enumerate(self.to):
                    scale = 1.0 if i == 0 else col("final_norm_w", m)
                    if m == 0:
                        self.tok[i] = ACT.op(lambda e: e.activation(to[:, :], XT[:, 0, :], ACTF.Square, scale=scale), tok,
                                             t_pb, *to.free)
                        continue
                    b = tmp.next()
                    t1 = ACT.op(lambda e: e.activation(b[:, :], XT[:, m, :], ACTF.Square, scale=scale), tok, *b.free)
                    self.tok[i] = DVE.op(lambda e: e.tensor_tensor(to[:, :], to[:, :], b[:, :], ALU.add), t1, self.tok[i])
                    b.free = [self.tok[i]]
                if m == KT - 1:
                    ACT.op(lambda e: e.activation(warm, EPS, ACTF.Sqrt), t_eps)

            def sums(self, i):
                bk, to = MB.next(), self.to[i]
                for c in range(NC):
                    tm = PE.op(lambda e: e.matmul(bk[:, c:c + 1], to[:, c * 128:(c + 1) * 128], ones[:, 0:1],
                                                  start=True, stop=True), self.tok[i], t_ones, *bk.free)
                to.free = [tm]
                return bk, tm

            def rstd(self, at):
                bk, tm = self.sums(0)
                t = ACT.op(lambda e: e.activation(small[:, at:at + 4], bk[:, 0:4], ACTF.Sqrt, bias=EPS, scale=1.0 / D),
                           tm, t_eps)
                bk.free = [t]
                return DVE.op(lambda e: e.reciprocal(small[:, at:at + 4], small[:, at:at + 4]), t)

        def spread(at, tok):
            q, bk = tmp.next(), MB.next()
            t = DVE.op(lambda e: e.tensor_tensor(q[:, :].rearrange("p (c t) -> p c t", c=NC),
                                                 ident[:, :].unsqueeze(1).to_broadcast([P, NC, P]),
                                                 small[:, at:at + 4].unsqueeze(2).to_broadcast([P, NC, P]), ALU.mult),
                       tok, t_id, *q.free)
            tm = PE.op(lambda e: e.matmul(bk[:, :], ones[:, :], q[:, :], start=True, stop=True), t, *bk.free)
            q.free = [tm]
            return bk, tm

        def split(src, tok, hi, lo, hfree=()):
            th = ACT.op(lambda e: e.activation(hi, src, ACTF.Copy), tok, *hfree)
            tl = DVE.op(lambda e: e.tensor_tensor(lo, src, hi.bitcast(F32), ALU.subtract), th, tok, *hfree)
            return (th, tl)

        def norm_splits(bank, rtok, scale, bias, stok, hfree):
            out, last = [], None
            for m in range(KT + 1):
                if m < KT:
                    b = tmp.next()
                    t1 = DVE.op(lambda e: e.scalar_tensor_tensor(out=b[:, :], in0=XT[:, m, :], scalar=scale(m),
                                                                 in1=bank[:, :], op0=ALU.mult, op1=ALU.mult),
                                xt_tok[m], rtok, stok, *b.free)
                    if bias is None:
                        th = ACT.op(lambda e: e.activation(Hh[:, m, :], b[:, :], ACTF.Copy), t1, *hfree)
                    else:
                        th = ACT.op(lambda e: e.activation(Hh[:, m, :], b[:, :], ACTF.Identity, bias=bias(m)), t1, *hfree)
                if last is not None:
                    j, q, tq = last
                    hi = Hh[:, j, :].bitcast(F32)
                    if bias is None:
                        tl = DVE.op(lambda e: e.tensor_tensor(Hl[:, j, :], q[:, :], hi, ALU.subtract), tq, *hfree)
                    else:
                        tl = DVE.op(lambda e: e.scalar_tensor_tensor(out=Hl[:, j, :], in0=q[:, :], scalar=bias(j), in1=hi,
                                                                     op0=ALU.add, op1=ALU.subtract), tq, *hfree)
                    q.free = [tl]
                    out.append((tq, tl))
                if m < KT:
                    last = (m, b, th)
            bank.free = [t1]
            return out

        done = object()
        xt_tok = [None] * KT

        if 1 in blocks:
            YB, = region(0, ("YB", [P, 16, T]))
            V, = region(32, ("V", [P, NC, D]))
            f2 = region(48, *((f"cfb{j}", [P, T]) for j in range(6)))
            YA, = region(48, ("YA", [P, KT, T]))
            (bsb, dts, bc, *stemps) = region(
                64, ("bsb", [P, KT, P]), ("dts", [P, 8, P]), ("bc", [P, 3, 32]),
                *((f"cfa{j}", [P, T]) for j in range(6)),
                *((f"xr{i}", [P, T + 3]) for i in range(2)),
                *((f"dec{i}", [P, T]) for i in range(2)),
                *((f"xdt{i}", [P, 256]) for i in range(2)),
                *((f"xd{i}", [P, 256]) for i in range(2)),
                *((f"xw{i}", [P, 256]) for i in range(2)),
                *((f"bn{i}", [P, 128]) for i in range(2)),
                ("yv", [P, NC, 256]), ("state", [P, 256]))
            wsT, wraw = region(74, ("wsT", [P, KT, P]), ("wraw", [P, KT, P]))
            GA, = region(82, ("GA", [P, KT, T]))
            GB, = region(32, ("GB", [P, KT, T]))
            R2h, R2l = region(48, ("R2h", [P, KT, T], F32R), ("R2l", [P, KT, T], F32R))
            YBh, YBl = region(0, ("YBh", [P, 16, T], F32R), ("YBl", [P, 16, T], F32R))

            sq_t = []
            for c in range(NC):
                t = ACT.op(lambda e, c=c: e.activation(xs[:, c, :], xnat[:, c, :], ACTF.Square,
                                                       accum_out=small[:, 4 + c:5 + c]), t_x)
                sq_t.append(t)
            ts = ACT.op(lambda e: e.activation(small[:, 4:8], small[:, 4:8], ACTF.Sqrt, bias=EPS, scale=1.0 / D),
                        sq_t[-1], t_eps)
            ts = DVE.op(lambda e: e.reciprocal(small[:, 4:8], small[:, 4:8]), ts)
            for c in range(NC):
                t_xs = DVE.op(lambda e, c=c: e.tensor_scalar(xs[:, c, :], xnat[:, c, :], small[:, 4 + c:5 + c], None,
                                                             ALU.mult), ts)
        t_pc = t_pb
        if 1 not in blocks:
            turn(2, pcC, rC, (s_par, 16 * 11))
            t_pc = tp[-1]
            tm = None
        if 1 in blocks:
            t_c = ACT.op(lambda e: e.activation(cact[:, :], colr("c", 0, 8), ACTF.Silu), t_pb)
        for m in range(KT):
            bk = BK[3 + m % 2]
            for c in range(NC):
                tm = PE.op(lambda e, m=m, c=c, bk=bk: e.transpose(bk[:, c * 128:(c + 1) * 128],
                                                                 xnat[:, c, m * 128:(m + 1) * 128], ident[:, :]),
                           t_x, t_id, *bk.free)
            xt_tok[m] = ACT.op(lambda e, m=m, bk=bk: e.activation(XT[:, m, :], bk[:, :], ACTF.Copy), tm)
            bk.free = [xt_tok[m]]
        t_xt = xt_tok[KT - 1]
        t_later = (s_par, 16 * 11)

        mac = Ring([Buf(t) for t in region(107, *((f"mac{i}", [P, P]) for i in range(2)))] if 1 in blocks else [])

        def mods(m):
            i, _ = take("mod")
            a, w = mac.next(), raw[i % NRAW].t
            t = POOL.op(lambda e: e.tensor_tensor(w[:, :, 0:P], w[:, :, 0:P], cact[:, :].unsqueeze(2).to_broadcast([P, KT, P]),
                                                  ALU.mult), ready[i], t_c)
            for n in (4, 2):
                t = POOL.op(lambda e: e.tensor_tensor(w[:, 0:n, 0:P], w[:, 0:n, 0:P], w[:, n:2 * n, 0:P], ALU.add), t)
            t = POOL.op(lambda e: e.tensor_tensor(a[:, :], w[:, 0, 0:P], w[:, 1, 0:P], ALU.add), t, *a.free)
            release(i, t)

            def total():
                bk = MB.next()
                tm = PE.op(lambda e: e.matmul(bk[:, 0:1], a[:, :], ones[:, 0:1], start=True, stop=True),
                           t, t_ones, *bk.free)
                a.free = [tm]
                ta = DVE.op(lambda e: e.tensor_tensor(modc[:, m:m + 1], bk[:, 0:1], colr("b_mod", m, 1), ALU.add), tm, t_pb)
                bk.free = [ta]
                return ta
            return total

        if 1 in blocks:
            MOD = dict(sh1=0, sc1=8, g1=16, sh2=24, sc2=32, g2=40)
            macc, = region(105, ("macc", [P, 256]))
            mrow, = region(68, ("mrow", [1, 1024]))
            bk, tm, t = BK[7], None, None
            rowb = BK[3:7]
            for i in range(8):
                if i % 2 == 0:
                    for k in range(KT):
                        w = wm[i][:, k, :]
                        if k == 0:
                            t = DVE.op(lambda e: e.tensor_scalar(macc[:, :], w, cact[:, 0:1], None, ALU.mult),
                                       (s_wm[i], 16), t_c, tm, *tp)
                        else:
                            t = DVE.op(lambda e: e.scalar_tensor_tensor(out=macc[:, :], in0=w, scalar=cact[:, k:k + 1],
                                                                        in1=macc[:, :], op0=ALU.mult, op1=ALU.add), t)
                else:
                    rb_ = rowb[i // 2]
                    o = rb_[0:1, 0:256]
                    for k in range(KT):
                        tr = PE.op(lambda e: e.matmul(o, cact[:, k:k + 1], wm[i][:, k, :], start=(k == 0),
                                                      stop=(k == KT - 1)), (s_wm[i], 16), t_c, *rb_.free)
                    trow = ACT.op(lambda e: e.activation(mrow[0:1, (i // 2) * 256:(i // 2) * 256 + 256], o, ACTF.Copy), tr)
                    rb_.free = [trow]
                    for j in range(2):
                        tm = PE.op(lambda e: e.matmul(bk[:, 2 * i - 2 + j:2 * i - 1 + j], macc[:, j * 128:(j + 1) * 128],
                                                      ones[:, 0:1], start=True, stop=True), t, t_ones, *bk.free)
            for i in range(1, 8, 2):
                for j in range(2):
                    q = (i // 2) * 256 + j * 128
                    tr = PE.op(lambda e: e.matmul(bk[:, 2 * i + j:2 * i + j + 1], mrow[0:1, q:q + 128],
                                                  ones[0:1, 0:1], start=True, stop=True), trow)
            t_mod = DVE.op(lambda e: e.tensor_tensor(modc[:, 0:16], bk[:, 0:16], colr("b_mod", 0, 16), ALU.add),
                           tm, tr, t_pb)
            bk.free = [t_mod]

            t_op = DVE.op(lambda e: e.tensor_scalar(opc[:, 0:8], modc[:, 8:16], 1.0, None, ALU.add), t_mod)
            htok = [None] * KT
            prep()
            prep()
            for m in range(KT):
                bk = BK[5 + m % 2]
                for c in range(NC):
                    tm = PE.op(lambda e, m=m, c=c, bk=bk: e.transpose(bk[:, c * 128:(c + 1) * 128],
                                                                     xs[:, c, m * 128:(m + 1) * 128], ident[:, :]),
                               t_xs, *bk.free)
                b = tmp.next()
                t1 = ACT.op(lambda e, m=m, bk=bk, b=b: e.activation(b[:, :], bk[:, :], ACTF.Identity,
                                                                   scale=opc[:, m:m + 1], bias=modc[:, m:m + 1]),
                            tm, t_op, *b.free)
                bk.free = [t1]
                htok[m] = split(b[:, :], t1, Hh[:, m, :], Hl[:, m, :])
                b.free = [*htok[m]]
            t_xdead = tm
            turn(0, pcA, 128, t_later, 0.5)
            turn(2, pcC, rC, t_later)
            t_cb = DVE.op(lambda e: e.tensor_scalar(colr("conv_b", 0, 32), colr("conv_b", 0, 32), 0.5, None, ALU.mult), t_pb)
            t_pc = tp[-1]

            s_bc = sem("s_bc")
            for i, name in enumerate(("dt_bias", "a_log", "d_skip")):
                SP.dma(lambda e, i=i, name=name: e.dma_start(bc[:, i, :], A[name].to_broadcast([P, 32])), s_bc, 0)
            SP.dma(lambda e: e.dma_start(bsb[:, :, :], A["gm_bs"].rearrange("a g i -> a (g i)").to_broadcast([P, D])
                                         .rearrange("p (g i) -> p g i", g=KT)), s_bc, 0, *tp)
            t_bc = (s_bc, 64)
            DT, AA, CU, NCU, EC, WE, EL, SC = (dts[:, i, :] for i in range(8))
            bd_, tm = gemm(Hh, Hl, htok)
            t_dtp = tm
            t5 = t7 = None
            t_dec = []

            def dt_steps(bd_, tm):
                nonlocal t5, t7
                q = tmp.next()
                t = ACT.op(lambda e: e.activation(q[0:32, :], bd_[0:32, :], ACTF.Copy), tm, *q.free)
                bd_.free = [t]
                bk = MB.next()
                for c in range(NC):
                    tm = PE.op(lambda e: e.transpose(bk[:, c * 32:(c + 1) * 32], q[0:32, c * 128:(c + 1) * 128],
                                                     ident[0:32, 0:32]), t, *bk.free)
                q.free = [tm]
                c4 = lambda ap: ap.rearrange("p (c h) -> p c h", c=NC)
                bcast = lambda i: bc[:, i, :].unsqueeze(1).to_broadcast([P, NC, 32])
                t = DVE.op(lambda e: e.tensor_tensor(c4(SC), c4(bk[:, 0:128]), bcast(0), ALU.add), tm, t_bc)
                bk.free = [t]
                yield
                t_al = ACT.op(lambda e: e.activation(bc[:, 1, :], bc[:, 1, :], ACTF.Exp), t_bc)
                t1 = ACT.op(lambda e: e.activation(DT, SC, ACTF.Abs), t)
                t1 = ACT.op(lambda e: e.activation(DT, DT, ACTF.Exp, scale=-1.0), t1)
                tu = DVE.op(lambda e: e.tensor_scalar(CU, DT, 1.0, None, ALU.add), t1)
                tl = ACT.op(lambda e: e.activation(AA, CU, ACTF.Ln), tu)
                td = DVE.op(lambda e: e.tensor_scalar(CU, CU, 1.0, None, ALU.subtract), tu, tl)
                tq = DVE.op(lambda e: e.tensor_scalar(NCU, CU, 0.0, None, ALU.is_equal), td)
                t2 = DVE.op(lambda e: e.tensor_tensor(AA, AA, NCU, ALU.add), tq, tl)
                t3 = DVE.op(lambda e: e.tensor_tensor(CU, CU, NCU, ALU.add), tq)
                t3 = DVE.op(lambda e: e.reciprocal(CU, CU), t3)
                t4 = DVE.op(lambda e: e.tensor_tensor(AA, AA, CU, ALU.mult), t2, t3)
                t4 = DVE.op(lambda e: e.tensor_tensor(AA, AA, DT, ALU.mult), t4)
                t_dt = DVE.op(lambda e: e.scalar_tensor_tensor(out=DT, in0=SC, scalar=0.0, in1=AA, op0=ALU.max, op1=ALU.add), t4)
                t5 = DVE.op(lambda e: e.scalar_tensor_tensor(out=c4(AA), in0=c4(DT), scalar=-1.0, in1=bcast(1),
                                                             op0=ALU.mult, op1=ALU.mult), t_dt, t_al)
                yield
                bk = BK[7]
                tm = PE.op(lambda e: e.matmul(bk[:, 0:128], triu[:, :], AA, start=True, stop=True), t5, t_triu, *bk.free)
                tm = PE.op(lambda e: e.matmul(bk[:, 128:256], ones[:, :], AA, start=True, stop=True))
                t6 = ACT.op(lambda e: e.activation(EC, bk[:, 0:128], ACTF.Exp), tm)
                t6 = ACT.op(lambda e: e.activation(EL, bk[:, 128:256], ACTF.Exp), tm)
                t7 = DVE.op(lambda e: e.tensor_scalar(NCU, bk[:, 0:128], -1.0, None, ALU.mult), tm, t6)
                t8 = DVE.op(lambda e: e.tensor_tensor(WE, bk[:, 128:256], NCU, ALU.add), t7)
                bk.free = [t8]
                t9 = ACT.op(lambda e: e.activation(WE, WE, ACTF.Exp), t8)
                t_dec[:] = [t_dt, t5, t7, t9]

            it = iter([Buf(t) for t in stemps])
            take_n = lambda n: [next(it) for _ in range(n)]
            cf = [take_n(6), [Buf(t) for t in f2]]
            xr, dec, xdt, xd, xw, bn = (Ring(take_n(2)) for _ in range(6))
            ca = tmp
            yv, state = take_n(2)
            for b in xr.bufs:
                t_xr0 = DVE.op(lambda e, b=b: e.memset(b[:, 0:3], 0.0))

            def conv(bk, tm, tile, dst):
                b, a = xr.next(), ca.next()
                t1 = ACT.op(lambda e: e.activation(b[:, 3:T + 3], bk[:, :], ACTF.Copy), tm, *b.free)
                t2 = ACT.op(lambda e: e.activation(a[:, :], bk[:, :], ACTF.Identity, scale=cw(3, tile),
                                                   bias=col("conv_b", tile)), tm, t_pc, t_cb, *a.free)
                bk.free = [t2]
                for tap in range(3):
                    t2 = DVE.op(lambda e, tap=tap: e.scalar_tensor_tensor(
                        out=a[:, :], in0=b[:, tap:tap + T], scalar=cw(tap, tile), in1=a[:, :],
                        op0=ALU.mult, op1=ALU.add), t1, t2, t_xr0)
                b.free = [t2]
                q = tmp.next()
                t3 = ACT.op(lambda e: e.activation(q[:, :], a[:, :], ACTF.Tanh), t2, *q.free)
                t3 = DVE.op(lambda e: e.scalar_tensor_tensor(out=dst[:, :], in0=q[:, :], scalar=1.0, in1=a[:, :],
                                                             op0=ALU.add, op1=ALU.mult), t3, *dst.free)
                a.free = q.free = [t3]
                return t3

            def ssd(g, F, ft):
                h4 = lambda ap: ap.rearrange("p (h d) -> p h d", h=4)
                colh = lambda ap, c: ap[:, c * 32 + g * 4:c * 32 + g * 4 + 4].unsqueeze(2).to_broadcast([P, 4, 64])
                ytok = []
                t_state = None
                d3 = lambda ap: ap.rearrange("p (h i) -> p h i", h=4)
                dsk = bc[:, 2, g * 4:g * 4 + 4].unsqueeze(2).to_broadcast([P, 4, 64])

                def open_chunk(c):
                    sl = slice(c * 128, (c + 1) * 128)
                    bs = BK[3]
                    PE.quiet(lambda e: e.matmul(d3(bs[:, :]), identb[:, :],
                                                maskb[:, :].unsqueeze(1).to_broadcast([P, 4, P]),
                                                start=True, stop=False, skip_group_check=True),
                             t_idb, t_mask, t5, *bs.free)
                    for h in range(4):
                        cc = c * 32 + g * 4 + h
                        tseg = PE.op(lambda e: e.matmul(bs[:, h * 128:(h + 1) * 128],
                                                        AA[:, cc:cc + 1].to_broadcast([P, P]), triu[:, :],
                                                        start=False, stop=(h == 3), skip_group_check=True))
                    bt, bcb = BK[4], BK[5]
                    for j in range(3):
                        tt = PE.op(lambda e: e.transpose(bt[:, j * 128:(j + 1) * 128], F[j][:, sl], ident[:, :]),
                                   ft[j], *bt.free)
                    tcb = PE.op(lambda e: e.matmul(bcb[:, 0:128], F[2][:, sl], F[3][:, sl], start=True, stop=True),
                                ft[2], ft[3], *bcb.free)
                    d = dec.next()
                    for h in range(4):
                        cc = c * 32 + g * 4 + h
                        td = ACT.op(lambda e: e.activation(d[:, h * 128:(h + 1) * 128], bs[:, h * 128:(h + 1) * 128],
                                                           ACTF.Exp, bias=NCU[:, cc:cc + 1]), tseg, t7, *d.free)
                    bs.free = [td]
                    a, b, w, n = xdt.next(), xd.next(), xw.next(), bn.next()
                    t1 = DVE.op(lambda e: e.tensor_tensor(h4(a[:, :]), h4(bt[:, 0:256]), colh(DT, c), ALU.mult),
                                tt, *t_dec, *a.free)
                    t2 = DVE.op(lambda e: e.tensor_tensor(h4(b[:, :]), h4(bt[:, 0:256]), dsk, ALU.mult), tt, t_bc, *b.free)
                    t3 = DVE.op(lambda e: e.tensor_tensor(h4(w[:, :]), h4(a[:, :]), colh(WE, c), ALU.mult), t1, *w.free)
                    t4 = ACT.op(lambda e: e.activation(n[:, :], bt[:, 256:384], ACTF.Copy), tt, t2, *n.free)
                    bt.free = [t4]
                    tM = DVE.op(lambda e: e.tensor_tensor(d3(d[:, :]), d3(d[:, :]),
                                                          bcb[:, 0:128].unsqueeze(1).to_broadcast([P, 4, P]), ALU.mult),
                                td, tcb)
                    bcb.free = [tM]
                    return d, a, b, w, n, t1, t2, t3, t4, tM

                opened = open_chunk(0)
                yield
                for c in range(NC):
                    sl = slice(c * 128, (c + 1) * 128)
                    d, a, b, w, n, t1, t2, t3, t4, tM = opened
                    if c < NC - 1:
                        opened = open_chunk(c + 1)
                        yield
                    by, bz = BK[6], BK[7]
                    for j in range(2):
                        tz = PE.op(lambda e: e.transpose(bz[:, j * 128:(j + 1) * 128], F[4 + j][:, sl], ident[:, :]),
                                   ft[4 + j], *bz.free)
                    if c < NC - 1:
                        tup = PE.op(lambda e: e.matmul(bz[:, 256:512], n[:, :], w[:, :], start=True, stop=True), t3, t4)
                    else:
                        tup = tz
                    for h in range(4):
                        tmm = PE.op(lambda e: e.matmul(by[:, h * 64:(h + 1) * 64], d[:, h * 128:(h + 1) * 128],
                                                       a[:, h * 64:(h + 1) * 64], start=True, stop=True),
                                    tM, t1, *by.free)
                    tin = tmm
                    if c > 0:
                        tin = PE.op(lambda e: e.matmul(by[:, 256:512], F[3][:, sl], state[:, :], start=True, stop=True),
                                    t_state)
                    d.free, a.free, n.free, w.free = [tmm], [tmm, t3], [tup], [tup]
                    if c == 0:
                        t_state = DVE.op(lambda e: e.tensor_copy(state[:, :], bz[:, 256:512]), tup, *state.free)
                    elif c < NC - 1:
                        s2 = DVE.op(lambda e: e.tensor_tensor(h4(state[:, :]), h4(state[:, :]), colh(EL, c), ALU.mult),
                                    tin, t_state)
                        t_state = DVE.op(lambda e: e.tensor_tensor(state[:, :], state[:, :], bz[:, 256:512], ALU.add),
                                         s2, tup)
                    else:
                        state.free = [tin]
                    yc = yv[:, c, :]
                    t6 = DVE.op(lambda e: e.tensor_tensor(yc, by[:, 0:256], b[:, :], ALU.add), tin, t2, *yv.free)
                    by.free = [t6]
                    if c > 0:
                        s1 = DVE.op(lambda e: e.tensor_tensor(h4(b[:, :]), h4(by[:, 256:512]), colh(EC, c), ALU.mult),
                                    tin, t6)
                        by.free = [s1]
                        t6 = DVE.op(lambda e: e.tensor_tensor(yc, yc, b[:, :], ALU.add), s1, t6)
                    t6 = DVE.op(lambda e: e.scalar_tensor_tensor(out=yc, in0=bz[:, 0:256], scalar=0.5, in1=yc,
                                                                 op0=ALU.mult, op1=ALU.mult), t6, tz, tup)
                    bz.free = [t6]
                    tq = DVE.op(lambda e: e.tensor_tensor_reduce(b[:, :], yc, yc, 1.0, 0.0, ALU.mult, ALU.add,
                                                                 small[:, 8 + c:9 + c]), t6)
                    b.free = [tq]
                    yield
                for j in range(6):
                    F[j].free = [tin, tz]
                ts = ACT.op(lambda e: e.activation(small[:, 12:16], small[:, 8:12], ACTF.Sqrt, bias=EPS,
                                                   scale=1.0 / 256), tq)
                ts = DVE.op(lambda e: e.reciprocal(small[:, 12:16], small[:, 12:16]), ts)
                for c in range(NC):
                    ts2 = DVE.op(lambda e, c=c: e.tensor_scalar(yv[:, c, :], yv[:, c, :], small[:, 12 + c:13 + c], None,
                                                               ALU.mult), ts)
                yield
                yield
                yield
                bz = BK[7]
                for j in range(2):
                    for c in range(NC):
                        tt = PE.op(lambda e, j=j, c=c: e.transpose(bz[:, c * 128:(c + 1) * 128],
                                                                   yv[:, c, j * 128:(j + 1) * 128], ident[:, :]),
                                   ts2, *bz.free)
                    t1 = ACT.op(lambda e, j=j: e.activation(YB[:, 2 * g + j, :], bz[:, :], ACTF.Copy,
                                                           scale=col("ssm_norm_w", 2 * g + j)), tt, t_xdead)
                    bz.free = [t1]
                    ybtok[2 * g + j] = t1
                    yield
                yv.free = [tt]
                ssd_done[:] = [tt, t1, ts2, tin]
                yield

            ybtok = [None] * 16
            ssd_done = []
            side = dt_steps(bd_, t_dtp)

            def steps(n):
                for _ in range(n):
                    if next(side, done) is done:
                        return

            step1 = lambda: steps(1)
            pending = []
            for g in range(8):
                F, ft = cf[g % 2], []
                for j, tile in enumerate((2 * g, 2 * g + 1, 16 + g, 24 + g)):
                    bk, tm = gemm(Hh, Hl, htok, hook=step1, every=3)
                    ft.append(conv(bk, tm, tile, F[j]))
                    if pending:
                        pending.pop()()
                    pending.append(mods(16 + 4 * g + j))
                for j in range(2):
                    bk, tm = gemm(Hh, Hl, htok, hook=step1, every=3)
                    q = tmp.next()
                    t = ACT.op(lambda e: e.activation(q[:, :], bk[:, :], ACTF.Tanh, scale=0.5), tm, *q.free)
                    t = DVE.op(lambda e: e.scalar_tensor_tensor(out=F[4 + j][:, :], in0=q[:, :], scalar=1.0, in1=bk[:, :],
                                                                op0=ALU.add, op1=ALU.mult), t, *F[4 + j].free)
                    bk.free = q.free = [t]
                    ft.append(t)
                steps(99)
                side = ssd(g, F, ft)
            t_modall = pending.pop()()
            t_op2 = DVE.op(lambda e: e.tensor_scalar(opc[:, 8:16], modc[:, 32:40], 1.0, None, ALU.add), t_modall)

            s_ws = sem("s_ws")
            vt = []
            for m in range(KT):
                bk, tm = gemm(Hh, Hl, htok, hook=step1, every=2)
                b = tmp.next()
                t1 = ACT.op(lambda e, bk=bk, b=b: e.activation(b[:, :], bk[:, :], ACTF.Gelu_apprx_tanh), tm, *b.free)
                bk.free = [t1]
                vt.append((b, t1, m))
                while vt and (len(vt) > 1 or m == KT - 1):
                    b, t1, mm = vt.pop(0)
                    bt = MB.next()
                    for c in range(NC):
                        tt = PE.op(lambda e, c=c, b=b, bt=bt: e.transpose(bt[:, c * 128:(c + 1) * 128],
                                                                  b[:, c * 128:(c + 1) * 128], ident[:, :]),
                                   t1, *bt.free)
                    b.free = [tt]
                    t_v = ACT.op(lambda e, mm=mm, bt=bt: e.activation(V[:, :, mm * 128:(mm + 1) * 128],
                                                              bt[:, :].rearrange("p (c d) -> p c d", c=NC), ACTF.Copy),
                                 tt)
                    bt.free = [t_v]
            steps(99)
            t_ws = SP.dma(lambda e: e.dma_start(wraw[:, :, :], A["gm_ws"][0].rearrange("g i j -> i g j")), s_ws, 16,
                          *ssd_done)
            for q in range(2):
                bk = BK[5 + q]
                for j in range(4):
                    tt = PE.op(lambda e, j=j, q=q, bk=bk: e.transpose(bk[:, j * 128:(j + 1) * 128],
                                                                     wraw[:, 4 * q + j, :], ident[:, :]),
                               t_ws, *bk.free)
                tc = DVE.op(lambda e, q=q, bk=bk: e.tensor_tensor(
                    wsT[:, 4 * q:4 * q + 4, :], bk[:, :].rearrange("p (g i) -> p g i", g=4),
                    triu[:, :].unsqueeze(1).to_broadcast([P, 4, P]), ALU.mult), tt, *ssd_done)
                bk.free = [tc]
            t_wsT = tc
            tv = None
            for c in range(NC):
                vq = wraw[:, :, :].rearrange("p g i -> p (g i)")
                tv = ACT.op(lambda e, c=c: e.activation(vq, V[:, c, :], ACTF.Square,
                                                        accum_out=small[:, 16 + c:17 + c]), t_v, tt, tv)
            ts = ACT.op(lambda e: e.activation(small[:, 16:20], small[:, 16:20], ACTF.Sqrt, bias=EPS, scale=1.0 / D), tv)
            ts = DVE.op(lambda e: e.reciprocal(small[:, 16:20], small[:, 16:20]), ts)
            for c in range(NC):
                tvs = DVE.op(lambda e, c=c: e.tensor_scalar(V[:, c, :], V[:, c, :], small[:, 16 + c:17 + c], None,
                                                           ALU.mult), ts, t_v)
            yatok = [None] * KT

            def sgu(m, u, t_u):
                bk = BK[3 + m % 2]
                for c in range(NC):
                    tt = PE.op(lambda e, c=c: e.matmul(bk[:, c * 128:(c + 1) * 128], V[:, c, m * 128:(m + 1) * 128],
                                                       wsT[:, m, :], start=True, stop=True), tvs, t_wsT, *bk.free)
                q = tmp.next()
                c3 = lambda ap: ap.rearrange("p (c i) -> p c i", c=NC)
                t1 = DVE.op(lambda e: e.scalar_tensor_tensor(
                    out=c3(q[:, :]), in0=c3(bk[:, :]), scalar=col("gm_norm_w", m),
                    in1=bsb[:, m, :].unsqueeze(1).to_broadcast([P, NC, P]), op0=ALU.mult, op1=ALU.add),
                    tt, t_bc, *q.free)
                bk.free = [t1]
                t2 = DVE.op(lambda e: e.tensor_tensor(YA[:, m, :], q[:, :], u[:, :], ALU.mult), t1, t_u)
                q.free = u.free = [t2]
                yatok[m] = t2
                return tt

            last = None
            for m in range(KT):
                bk, tm = gemm(Hh, Hl, htok)
                if last:
                    sgu(*last)
                u = tmp.next()
                t1 = ACT.op(lambda e, bk=bk, u=u: e.activation(u[:, :], bk[:, :], ACTF.Gelu_apprx_tanh), tm, *u.free)
                bk.free = [t1]
                last = (m, u, t1)
            t_vdead = sgu(*last)

            gtok = [[], []]
            for br, (G, gdead) in enumerate(((GA, ssd_done), (GB, [t_vdead]))):
                for m in range(KT):
                    bk, tm = gemm(Hh, Hl, htok)
                    t1 = ACT.op(lambda e, bk=bk, G=G, m=m: e.activation(G[:, m, :], bk[:, :], ACTF.Sigmoid), tm, *gdead)
                    bk.free = [t1]
                    gtok[br].append(t1)
            ya2 = [split(YA[:, m, :], yatok[m], Hh[:, m, :], Hl[:, m, :], [tm]) for m in range(KT)]
            yb2 = [split(YB[:, 8 + m, :], ybtok[8 + m], R2h[:, m, :], R2l[:, m, :], [ya2[-1][0], ya2[-1][1], t_vdead])
                   for m in range(KT)]
            mtok = [None] * KT
            for m in range(KT):
                bk, tm = gemm(Hh, Hl, ya2)
                mtok[m] = DVE.op(lambda e, bk=bk, m=m: e.tensor_tensor(GA[:, m, :], GA[:, m, :], bk[:, :], ALU.mult),
                                 tm, gtok[0][m])
                bk.free = [mtok[m]]
            yb1 = [split(YB[:, m, :], ybtok[m], Hh[:, m, :], Hl[:, m, :], [tm]) for m in range(KT)]
            mm_tok = []
            for X_h, X_l, xt in ((R2h, R2l, yb2), (Hh, Hl, yb1)):
                for m in range(KT):
                    bk, tm = gemm(X_h, X_l, xt)
                    q = tmp.next()
                    t2 = DVE.op(lambda e, bk=bk, q=q, m=m: e.tensor_tensor(q[:, :], GB[:, m, :], bk[:, :], ALU.mult), tm,
                                gtok[1][m], *q.free)
                    bk.free = [t2]
                    mtok[m] = DVE.op(lambda e, q=q, m=m: e.tensor_tensor(GA[:, m, :], GA[:, m, :], q[:, :], ALU.add), t2,
                                     mtok[m])
                    q.free = [mtok[m]]
                    if X_h is Hh:
                        mm_tok.append(split(GA[:, m, :], mtok[m], R2h[:, m, :], R2l[:, m, :], [t_r2dead]))
                t_r2dead = tm
            t_hdead = tm
            t_ydead = tm
            rows = Rows(1)
            for m in range(KT):
                bk, tm = gemm(R2h, R2l, mm_tok)
                t1 = DVE.op(lambda e, bk=bk, m=m: e.scalar_tensor_tensor(
                    out=XT[:, m, :], in0=bk[:, :], scalar=modc[:, 16 + m:17 + m], in1=XT[:, m, :],
                    op0=ALU.mult, op1=ALU.add), tm, t_modall, xt_tok[m])
                bk.free = [t1]
                xt_tok[m] = t1
                rows.add(m, t1)
            t_rs = rows.rstd(24)
            nb, t_r = spread(24, t_rs)
            h2 = norm_splits(nb, t_r, lambda m: opc[:, 8 + m:9 + m], lambda m: modc[:, 24 + m:25 + m], t_op2, [t_hdead])
            fdead = mtok[-1]
            for f in range(2):
                ftok = []
                for m in range(16):
                    bk, tm = gemm(Hh, Hl, h2)
                    t_hdead = tm
                    q = tmp.next()
                    t1 = ACT.op(lambda e, bk=bk, q=q: e.activation(q[:, :], bk[:, :], ACTF.Relu), tm, *q.free)
                    bk.free = [t1]
                    t2 = DVE.op(lambda e, q=q: e.tensor_tensor(q[:, :], q[:, :], q[:, :], ALU.mult), t1)
                    ftok.append(split(q[:, :], t2, YBh[:, m, :], YBl[:, m, :], [fdead]))
                    q.free = [*ftok[-1]]
                if f == 1:
                    rows = Rows(2)
                for m in range(KT):
                    bk, tm = gemm(YBh, YBl, ftok, 2)
                    fdead = tm
                    t1 = DVE.op(lambda e, bk=bk, m=m: e.scalar_tensor_tensor(
                        out=XT[:, m, :], in0=bk[:, :], scalar=modc[:, 40 + m:41 + m], in1=XT[:, m, :],
                        op0=ALU.mult, op1=ALU.add), tm, t_modall, xt_tok[m])
                    bk.free = [t1]
                    xt_tok[m] = t1
                    if f == 1:
                        rows.add(m, t1)

        if 2 in blocks:
            if 1 not in blocks:
                t_r = None
            H2 = lambda: None
            names = [("KR0", [P, NC, 2, P]), ("KR1", [P, NC, 2, P]), ("bt0", [P, T]), ("bt1", [P, T]),
                     ("kt0", [P, T]), ("kt1", [P, T]), ("VT", [P, T]), ("Vn", [P, T]), ("KKn", [P, T]), ("Bn", [P, T]),
                     ("Kn", [P, T])]
            for h in range(2):
                names += [(f"{n}{h}", [P, T]) for n in ("Ln", "Xx", "Tt", "AU", "RB", "RK")]
            names += [("Ww0", [P, T]), ("Ww1", [P, T]), ("Qt", [P, T]), ("Gg", [P, T]), ("AV0", [P, 256]), ("AV1", [P, 256]),
                      ("Uu0", [P, P]), ("Uu1", [P, P]), ("Sbd", [P, P]), ("Sf", [P, P])]
            names += [(f"wk{i}", [P, T]) for i in range(5)]
            names += [("Y", [P, KT, T]), ("YT", [P, T]), ("GT", [P, T]), ("BO", [P, T])]
            names += [(f"pad{i}", [P, T + 16]) for i in range(3)]
            names += [("LR", [P, T]), ("WU", [P, T]), ("PW", [P, T]), ("bd", [P, P]), ("fx0", [P, 16]), ("fx1", [P, 16]),
                      ("rc", [P, 16]), ("omka", [P, 4]), ("mt", [P, P])]
            names += [(f"msk{i}", [P, P], mybir.dt.uint8) for i in range(11)]
            Z = {n[0]: t for n, t in zip(names, region(0, *names))}
            B2 = {n: Buf(t) for n, t in Z.items()}
            if 1 not in blocks:
                fdead = tm
            dead = [fdead, *xt_tok]
            s_w2 = sem("s_w2")
            SP.dma(lambda e: e.dma_start(Z["WU"][0:64, :], A["w_up_2"][0]), s_w2, 0, *dead)
            SP.dma(lambda e: e.dma_start(Z["WU"][64:128, :], A["a_up_2"][0]), s_w2, 0)
            SP.dma(lambda e: e.dma_start(Z["PW"][:, :].rearrange("p (g d) -> p g d", g=4),
                                         A["pool_w_2"][0].rearrange("g c d -> c g d")), s_w2, 0)
            t_w2 = (s_w2, 48)

            mt = Z["mt"]
            t_c0 = None
            for i in range(16):
                t_c0 = POOL.op(lambda e: e.memset(Z["rc"][:, i:i + 1], 1.0 / (i + 1)), *dead)
            for i in range(3):
                t_c0 = POOL.op(lambda e: e.memset(Z[f"pad{i}"][:, 0:16], 0.0))
            for h in range(2):
                for n in ("Ln", "AU", "RB", "RK"):
                    t_c0 = POOL.op(lambda e: e.memset(Z[f"{n}{h}"][:, :], 0.0))
            t_c0 = POOL.op(lambda e: e.memset(Z["Sbd"][:, :], 0.0))
            t_bd = POOL.op(lambda e: e.memset(Z["bd"][:, :], 0.0), *dead)
            t_bd = POOL.op(lambda e: e.memset(Z["bd"][0:64, 0:64], 1.0), t_bd)
            t_bd = POOL.op(lambda e: e.memset(Z["bd"][64:128, 64:128], 1.0), t_bd)
            t_m = t_bd
            LEVELS = [1, 2, 4, 8, 16, 32, 64]
            MX = []
            for q, n in enumerate(LEVELS):
                t_m = POOL.op(lambda e: e.memset(mt[:, :], 0.0), t_m)
                mv = mt[:, :].rearrange("p (b h j) -> p b h j", h=2, j=n)[:, :, 1, :]
                nb = P // (2 * n)
                t_m = POOL.op(lambda e: e.memset(mv, 1.0), t_m)
                t_m = POOL.op(lambda e: e.affine_select(out=mv, in_=mv, compare_op=ALU.is_ge, fill=0.0, base=0,
                                                        pattern=[[-2 * n, nb], [0, n]], channel_multiplier=1), t_m)
                t_m = POOL.op(lambda e: e.affine_select(out=mv, in_=mv, compare_op=ALU.is_ge, fill=0.0, base=n - 1,
                                                        pattern=[[2 * n, nb], [0, n]], channel_multiplier=-1), t_m)
                m8 = Z[f"msk{q}"]
                t_m = POOL.op(lambda e: e.tensor_copy(m8[:, :], mt[:, :]), t_m)
                MX.append(m8)
            t_m = POOL.op(lambda e: e.memset(mt[:, :], 0.0), t_m)
            mv = mt[:, :].rearrange("p (b h) -> p b h", h=2)[:, :, 0]
            t_m = POOL.op(lambda e: e.affine_select(out=mv, in_=mv, compare_op=ALU.not_equal, fill=1.0, base=-1,
                                                    pattern=[[-2, 64]], channel_multiplier=1), t_m)
            t_m = POOL.op(lambda e: e.tensor_copy(Z["msk7"][:, :], mt[:, :]), t_m)
            for q, base, step, mult in ((8, -1, -1, 1), (9, -1, 1, -1), (10, 0, 1, -1)):
                t_m = POOL.op(lambda e: e.affine_select(out=mt[:, :], in_=ones[:, :], compare_op=ALU.is_ge, fill=0.0,
                                                        base=base, pattern=[[step, P]], channel_multiplier=mult), t_m)
                t_m = POOL.op(lambda e: e.tensor_copy(Z[f"msk{q}"][:, :], mt[:, :]), t_m)
            M_LN1, M_LO, M_SU, M_U = (Z[f"msk{q}"] for q in (7, 8, 9, 10))
            if 1 in blocks:
                t_r1 = rows.rstd(24)
                bk, tm = rows.sums(1)
                sc4 = lambda i: small[:, 24 + 4 * i:28 + 4 * i]
                t = DVE.op(lambda e: e.tensor_tensor(sc4(1), bk[:, 0:4], sc4(0), ALU.mult), tm, t_r1)
                bk.free = [t]
                t = DVE.op(lambda e: e.tensor_tensor(sc4(1), sc4(1), sc4(0), ALU.mult), t)
                t = ACT.op(lambda e: e.activation(sc4(1), sc4(1), ACTF.Sqrt, bias=EPS, scale=1.0 / D), t)
                t = DVE.op(lambda e: e.reciprocal(sc4(1), sc4(1)), t)
                t = DVE.op(lambda e: e.tensor_tensor(sc4(1), sc4(1), sc4(0), ALU.mult), t)
                nb, t_r = spread(28, t)
                t_wg = DVE.op(lambda e: e.tensor_tensor(opc[:, 0:8], colr("final_norm_w", 0, 8),
                                                        colr("norm_gain_2", 0, 8), ALU.mult), t_pb, htok[-1][0])
                h3 = norm_splits(nb, t_r, lambda m: opc[:, m:m + 1], None, t_wg, [t_hdead])
                nb, t_r = spread(24, t_r1)
                for m in range(KT):
                    xt_tok[m] = DVE.op(lambda e: e.scalar_tensor_tensor(
                        out=XT[:, m, :], in0=XT[:, m, :], scalar=col("final_norm_w", m), in1=nb[:, :],
                        op0=ALU.mult, op1=ALU.mult), xt_tok[m], t_r)
                nb.free = [xt_tok[-1]]
            else:
                rows = Rows(1)
                for m in range(KT):
                    rows.add(m, xt_tok[m])
                nb, t_r = spread(24, rows.rstd(24))
                h3 = norm_splits(nb, t_r, lambda m: col("norm_gain_2", m), None, t_pb, [])
            t_c0 = DVE.op(lambda e: e.tensor_scalar(Z["omka"][:, :], colr("k_a_2", 0, 4), -1.0, 1.0, ALU.mult, ALU.add),
                         t_pc, t_c0)
            wk = Stock([B2[f"wk{i}"] for i in range(5)] + [acc, rb])
            pads = Ring([B2[f"pad{i}"] for i in range(3)])
            c4_ = lambda ap: ap.rearrange("p (c t) -> p c t", c=NC)
            bd = Z["bd"]
            L = EM05

            def shift(bk, tm, tile, dst):
                b, d = pads.next(), tmp.next()
                t1 = ACT.op(lambda e: e.activation(b[:, 16:], bk[:, :], ACTF.Copy), tm, t_c0, *b.free)
                bk.free = [t1]
                t2 = DVE.op(lambda e: e.tensor_tensor(d[:, :], b[:, 15:T + 15], b[:, 16:], ALU.subtract), t1, *d.free)
                t3 = DVE.op(lambda e: e.scalar_tensor_tensor(out=dst[:, :], in0=d[:, :], scalar=col("shift_mu_2", tile),
                                                             in1=b[:, 16:], op0=ALU.mult, op1=ALU.add),
                            t2, t_pc, *dst.free)
                b.free = d.free = [t3]
                return t3

            def head_sums(src, tok):
                bk = MB.next()
                tm = PE.op(lambda e: e.matmul(bk[:, :], bd[:, :], src, start=True, stop=True), tok, t_bd, *bk.free)
                return bk, tm

            bk, tm = gemm(Hh, Hl, h3)
            LR = B2["LR"]
            t_lr = shift(bk, tm, 12, LR)
            t_lr = ACT.op(lambda e: e.activation(LR[0:64, :], LR[0:64, :], ACTF.Tanh), t_lr)

            sets = [dict(KR=B2[f"KR{i}"], bt=B2[f"bt{i}"], kt=B2[f"kt{i}"], fx=B2[f"fx{i}"]) for i in range(2)]
            cur = {}

            def decays(f):
                s = cur[f] = dict(sets[f % 2])
                fx = s["fx"]
                sg, a, cs, ip = (wk.get() for _ in range(4))
                out2 = []
                for q, dst, name in ((0, sg, "w0_2"), (64, a, "a0_2")):
                    bk = MB.next()
                    tm = PE.op(lambda e: e.matmul(bk[:, :], Z["WU"][q:q + 64, f * 128:(f + 1) * 128], LR[q:q + 64, :],
                                                  start=True, stop=True), t_lr, t_w2, *bk.free)
                    t = ACT.op(lambda e: e.activation(dst[:, :], bk[:, :], ACTF.Sigmoid, bias=col(name, f)), tm, t_pc,
                               *dst.free)
                    bk.free = [t]
                    out2.append(t)
                t_sg, s["ta"] = out2
                for c in range(NC):
                    sl = slice(c * 128, (c + 1) * 128)
                    t1 = DVE.op(lambda e: e.tensor_tensor_scan(cs[:, sl], ones[:, :], sg[:, sl], 0.0, ALU.mult, ALU.add),
                                t_sg, t_ones, *cs.free)
                t2 = DVE.op(lambda e: e.tensor_copy(fx[:, 0:4], c4_(cs[:, :])[:, :, 63]), t1, *fx.free)
                t3 = DVE.op(lambda e: e.tensor_tensor(c4_(cs[:, :]), c4_(cs[:, :]),
                                                      fx[:, 0:4].unsqueeze(2).to_broadcast([P, NC, P]), ALU.subtract), t2)
                t4 = DVE.op(lambda e: e.tensor_tensor(sg[:, :], cs[:, :], sg[:, :], ALU.subtract), t3)
                t5 = ACT.op(lambda e: e.activation(fx[:, 4:8], fx[:, 0:4], ACTF.Exp, scale=-L), t2)
                t5 = ACT.op(lambda e: e.activation(fx[:, 8:12], c4_(cs[:, :])[:, :, 127], ACTF.Exp, scale=-L), t3)
                s["tfac"] = DVE.op(lambda e: e.tensor_tensor(fx[:, 12:15], fx[:, 8:11], fx[:, 5:8], ALU.mult), t5)
                s["tip"] = ACT.op(lambda e: e.activation(ip[:, :], cs[:, :], ACTF.Exp, scale=L), t3, *ip.free)
                s["trp"] = ACT.op(lambda e: e.activation(cs[:, :], cs[:, :], ACTF.Exp, scale=-L), t5, t4)
                s["tpp"] = ACT.op(lambda e: e.activation(sg[:, :], sg[:, :], ACTF.Exp, scale=-L), t4)
                s.update(pp=sg, a=a, rp=cs, ip=ip)

            def keys(f, bk, tm):
                s = cur[f]
                k, kk = wk.get(), wk.get()
                tk = shift(bk, tm, 4 + f, k)
                t1 = DVE.op(lambda e: e.tensor_scalar(kk[:, :], k[:, :], col("k_k_2", f), None, ALU.mult), tk, *kk.free)
                q = tmp.next()
                t2 = ACT.op(lambda e: e.activation(q[:, :], kk[:, :], ACTF.Square), t1, *q.free)
                for _ in range(4):
                    yield
                b, tm = head_sums(q[:, :], t2)
                t3 = ACT.op(lambda e: e.activation(q[:, :], b[:, :], ACTF.Sqrt), tm)
                b.free = [t3]
                t3 = DVE.op(lambda e: e.tensor_scalar(q[:, :], q[:, :], 1e-12, None, ALU.max), t3)
                t3 = DVE.op(lambda e: e.reciprocal(q[:, :], q[:, :]), t3)
                t3 = DVE.op(lambda e: e.tensor_tensor(kk[:, :], kk[:, :], q[:, :], ALU.mult), t3, t1)
                t4 = DVE.op(lambda e: e.tensor_scalar(q[:, :], s["a"][:, :], col("k_a_2", f), Z["omka"][:, f:f + 1],
                                                      ALU.mult, ALU.add), s["ta"], t3)
                t4 = DVE.op(lambda e: e.tensor_tensor(k[:, :], k[:, :], q[:, :], ALU.mult), t4)
                q.free = [t4]
                KR = s["KR"]
                t5 = DVE.op(lambda e: e.scalar_tensor_tensor(out=KR[:, :, 0, :], in0=c4_(kk[:, :]), scalar=-1.0,
                                                             in1=c4_(s["pp"][:, :]), op0=ALU.mult, op1=ALU.mult),
                            t3, s["tpp"], *KR.free)
                t6 = DVE.op(lambda e: e.tensor_tensor(kk[:, :], kk[:, :], s["a"][:, :], ALU.mult), t5, s["ta"])
                t6 = DVE.op(lambda e: e.tensor_tensor(s["bt"][:, :], kk[:, :], s["ip"][:, :], ALU.mult), t6, s["tip"],
                            *s["bt"].free)
                t7 = DVE.op(lambda e: e.tensor_tensor(s["kt"][:, :], k[:, :], s["ip"][:, :], ALU.mult), t4,
                            *s["kt"].free)
                s.update(tkk=t5, tb=t6, tkt=t7, k2=k, tk2=t4)
                wk.give(kk, t6)
                wk.give(s["pp"], t5)
                wk.give(s["a"], t6)
                wk.give(s["ip"], t7)

            def receptance(f, bk, tm):
                s = cur[f]
                r = wk.get()
                tr = shift(bk, tm, f, r)
                s["tr"] = DVE.op(lambda e: e.tensor_tensor(s["KR"][:, :, 1, :], c4_(r[:, :]), c4_(s["rp"][:, :]), ALU.mult),
                                 tr, s["trp"], *s["KR"].free)
                t2 = DVE.op(lambda e: e.scalar_tensor_tensor(out=r[:, :], in0=r[:, :], scalar=col("r_k_2", f),
                                                             in1=s["k2"][:, :], op0=ALU.mult, op1=ALU.mult),
                            s["tr"], s["tk2"])
                wk.give(s["rp"], s["tr"])
                wk.give(s["k2"], t2, s["tkt"])
                s.update(rk=r, trk=t2)

            def values(f, bk, tm):
                s = cur[f]
                V2, BO = B2["VT"], B2["BO"]
                s["tv"] = shift(bk, tm, 8 + f, V2)
                b, tm = head_sums(s["rk"][:, :], s["trk"])
                wk.give(s["rk"], tm)
                s["tbo"] = DVE.op(lambda e: e.tensor_tensor(BO[:, :], V2[:, :], b[:, :], ALU.mult), tm, s["tv"], *BO.free)
                b.free = [s["tbo"]]

            R4 = lambda ap: ap.rearrange("p (c t) -> p c t", c=NC)
            m4 = lambda m: m[:, :].unsqueeze(1).to_broadcast([P, NC, P])

            def head(f, hp, res):
                s = cur[f]
                b0, b1 = BK[3 + 2 * hp], BK[4 + 2 * hp]
                rows = slice(64 * hp, 64 * hp + 64)
                Ln, Xx, Tt, AU, RB, RK = (B2[f"{n}{hp}"] for n in ("Ln", "Xx", "Tt", "AU", "RB", "RK"))
                t_tT = t_x0 = None
                tg = {}
                gt = (s["tkk"], s["tb"], s["tkt"], s["tr"])
                ti = ACT.op(lambda e: e.activation(R4(Xx[:, :]), ident[:, :].unsqueeze(1).to_broadcast([P, NC, P]),
                                                   ACTF.Copy), t_id, *Xx.free)
                tj = ACT.op(lambda e: e.activation(R4(Tt[:, :]), ident[:, :].unsqueeze(1).to_broadcast([P, NC, P]),
                                                   ACTF.Copy), t_id, *Tt.free)
                pair = 0
                for left, o0, m0, o1, m1 in (("bt", None, None, RB, M_U), ("kt", AU, M_SU, RK, M_U)):
                    for half in range(2):
                        bk = (b0, b1)[half]
                        for cc in range(2):
                            c = 2 * half + cc
                            tg = PE.op(lambda e: e.matmul(bk[:, cc * 256:(cc + 1) * 256].rearrange("p (a t) -> p a t", a=2),
                                                          s[left][rows, c * 128:(c + 1) * 128], s["KR"][rows, c, :, :],
                                                          start=True, stop=True), *gt, *bk.free)
                        v = bk[:, :].rearrange("p (c a t) -> p c a t", c=2, a=2)
                        hs = slice(2 * half, 2 * half + 2)
                        m2 = lambda m: m[:, :].unsqueeze(1).to_broadcast([P, 2, P])
                        if o0 is None:
                            t1 = DVE.op(lambda e: e.copy_predicated(R4(Xx[:, :])[:, hs, :], m2(MX[0]), v[:, :, 0, :]),
                                        tg, ti, t_m)
                        else:
                            t1 = DVE.op(lambda e: e.copy_predicated(R4(o0[:, :])[:, hs, :], m2(m0), v[:, :, 0, :]),
                                        tg, t_m, t_c0, *o0.free)
                        t2 = DVE.op(lambda e: e.copy_predicated(R4(o1[:, :])[:, hs, :], m2(m1), v[:, :, 1, :]),
                                    tg, t_m, t_c0, *o1.free)
                        bk.free = [t2, t1]
                        if o0 is None:
                            t_x = t1
                            t_rb = t2
                        else:
                            t_au, t_rk = t1, t2
                    yield
                for c in range(NC):
                    tg = PE.op(lambda e: e.matmul(b0[:, c * 128:(c + 1) * 128], s["KR"][rows, c, 0, :],
                                                  s["bt"][rows, c * 128:(c + 1) * 128], start=True, stop=True),
                               *b0.free)
                t1 = DVE.op(lambda e: e.copy_predicated(R4(Tt[:, :]), m4(M_LN1), R4(b0[:, :])), tg, tj, t_m)
                t_ln = DVE.op(lambda e: e.copy_predicated(R4(Ln[:, :]), m4(M_LO), R4(b0[:, :])), tg, t_c0, t_m, *Ln.free)
                b0.free = [t_ln]
                t_t = t1
                yield
                w = B2[f"Ww{hp}"]
                for q in range(1, 7):
                    for c in range(NC):
                        sl = slice(c * 128, (c + 1) * 128)
                        tw = PE.op(lambda e: e.matmul(b0[:, sl], Ln[:, sl], Xx[:, sl], start=True, stop=True),
                                   t_ln, t_x, *b0.free)
                    tw = ACT.op(lambda e: e.activation(w[:, :], b0[:, :], ACTF.Copy), tw, *w.free)
                    b0.free = [tw]
                    yield
                    for c in range(NC):
                        sl = slice(c * 128, (c + 1) * 128)
                        tx = PE.op(lambda e: e.matmul(b1[:, sl], Tt[:, sl], w[:, sl], start=True, stop=True),
                                   tw, t_t, *b1.free)
                    w.free = [tx]
                    t_x = DVE.op(lambda e: e.copy_predicated(R4(Xx[:, :]), m4(MX[q]), R4(b1[:, :])), tx)
                    b1.free = [t_x]
                    yield
                    if q < 6:
                        for c in range(NC):
                            sl = slice(c * 128, (c + 1) * 128)
                            tt = PE.op(lambda e: e.transpose(b1[:, sl], Xx[:, sl], ident[:, :]), t_x, *b1.free)
                        t_t = ACT.op(lambda e: e.activation(Tt[:, :], b1[:, :], ACTF.Copy), tt)
                        b1.free = [t_t]
                res.update({("x", hp): t_x, ("au", hp): t_au, ("rb", hp): t_rb, ("rk", hp): t_rk})
                Ln.free = [tw]
                Tt.free = [tx]

            def rwkv(f):
                s = cur[f]
                KR = s["KR"]
                Vn, KKn, Bn, Kn, YT, GT, BO = (B2[n] for n in ("Vn", "KKn", "Bn", "Kn", "YT", "GT", "BO"))
                Qt, G, Sbd, Sf = (B2[n] for n in ("Qt", "Gg", "Sbd", "Sf"))
                bs = BK[7]
                nat = {}
                for n, dst, src, tok in (("v", Vn, lambda c: B2["VT"][:, c * 128:(c + 1) * 128], s["tv"]),
                                         ("kk", KKn, lambda c: KR[:, c, 0, :], s["tkk"]),
                                         ("b", Bn, lambda c: s["bt"][:, c * 128:(c + 1) * 128], s["tb"]),
                                         ("k", Kn, lambda c: s["kt"][:, c * 128:(c + 1) * 128], s["tkt"])):
                    for c in range(NC):
                        tt = PE.op(lambda e: e.transpose(bs[:, c * 128:(c + 1) * 128], src(c), ident[:, :]), tok, *bs.free)
                    if n == "v":
                        B2["VT"].free = [tt, s["tbo"]]
                    nat[n] = ACT.op(lambda e: e.activation(dst[:, :], bs[:, :], ACTF.Copy), tt, *dst.free)
                    bs.free = [nat[n]]
                    yield
                res = {}
                gens = [head(f, 0, res), head(f, 1, res)]
                while gens:
                    for g in list(gens):
                        if next(g, done) is done:
                            gens.remove(g)
                        yield
                av, tg = [B2["AV0"], B2["AV1"]], []
                for hp in range(2):
                    b0 = BK[3 + 2 * hp]
                    for c in range(NC):
                        tm = PE.op(lambda e: e.matmul(b0[:, c * 64:(c + 1) * 64], B2[f"AU{hp}"][:, c * 128:(c + 1) * 128],
                                                      Vn[:, c * 128 + 64 * hp:c * 128 + 64 * hp + 64],
                                                      start=True, stop=True), res[("au", hp)], nat["v"], *b0.free)
                    t = DVE.op(lambda e: e.tensor_copy(av[hp][:, :], b0[:, 0:256]), tm, *av[hp].free)
                    b0.free = [t]
                    tg.append(t)
                    B2[f"AU{hp}"].free = [tm]
                yield
                b1 = BK[4]
                for hp in range(2):
                    for c in range(NC):
                        tq = PE.op(lambda e: e.matmul(b1[64 * hp:64 * hp + 64, c * 128:(c + 1) * 128],
                                                      KKn[:, c * 128 + 64 * hp:c * 128 + 64 * hp + 64],
                                                      B2[f"Xx{hp}"][:, c * 128:(c + 1) * 128], start=True, stop=True),
                                   res[("x", hp)], nat["kk"], *b1.free)
                t_q = ACT.op(lambda e: e.activation(Qt[:, :], b1[:, :], ACTF.Copy), tq, *Qt.free)
                b1.free = [t_q]
                KKn.free = [tq]
                b1 = BK[6]
                for hp in range(2):
                    for c in range(NC):
                        tq = PE.op(lambda e: e.matmul(b1[:, c * 128 + 64 * hp:c * 128 + 64 * hp + 64],
                                                      B2[f"Xx{hp}"][:, c * 128:(c + 1) * 128],
                                                      av[hp][:, c * 64:(c + 1) * 64], start=True, stop=True),
                                   tg[hp], *b1.free)
                    av[hp].free = [tq]
                    B2[f"Xx{hp}"].free = [tq]
                t_g = ACT.op(lambda e: e.activation(G[:, :], b1[:, :], ACTF.Copy), tq, *G.free)
                b1.free = [t_g]
                yield
                t_s = None
                for c in range(NC):
                    sl = slice(c * 128, (c + 1) * 128)
                    by, bu = BK[3], BK[5]
                    if c == 0:
                        U, t_u, uof = G, t_g, 0
                        Ua = G[:, 0:128]
                    else:
                        Ub = B2[f"Uu{c % 2}"]
                        Ua = Ub[:, :]
                        tm = PE.op(lambda e: e.matmul(bu[:, 0:128], Qt[:, sl], Sbd[:, :], start=True, stop=True),
                                   t_q, t_s, *bu.free)
                        t_u = DVE.op(lambda e: e.tensor_tensor(Ua, bu[:, 0:128], G[:, sl], ALU.add), tm, t_g, *Ub.free)
                        bu.free = [t_u]
                        tf = None
                        if c < NC - 1:
                            tf = DVE.op(lambda e: e.tensor_scalar(Sf[:, :], Sbd[:, :], s["fx"][:, 12 + c:13 + c], None,
                                                                  ALU.mult), t_s, s["tfac"])
                        yield
                    if c < NC - 1:
                        bq = BK[4]
                        tm = PE.op(lambda e: e.matmul(bq[:, 0:128], Kn[:, sl], Vn[:, sl], start=True, stop=False),
                                   nat["k"], nat["v"], *bq.free)
                        tm = PE.op(lambda e: e.matmul(bq[:, 0:128], Bn[:, sl], Ua, start=False, stop=True), nat["b"], t_u)
                    if c > 0:
                        ty = PE.op(lambda e: e.matmul(by[:, 0:128], Sbd[:, :], KR[:, c, 1, :], start=True, stop=False,
                                                      skip_group_check=True), t_s, *by.free)
                    for hp in range(2):
                        vs = slice(64 * hp, 64 * hp + 64)
                        ty = PE.op(lambda e: e.matmul(by[vs, 0:128], Vn[:, c * 128 + 64 * hp:c * 128 + 64 * hp + 64],
                                                      B2[f"RK{hp}"][:, sl], start=(c == 0), stop=False,
                                                      skip_group_check=True), res[("rk", hp)], nat["v"], *by.free)
                        ty = PE.op(lambda e: e.matmul(by[vs, 0:128], Ua[:, vs], B2[f"RB{hp}"][:, sl], start=False,
                                                      stop=True, skip_group_check=True), res[("rb", hp)], t_u)
                    if c > 0:
                        Ub.free = [ty]
                    if c < NC - 1:
                        for hp in range(2):
                            vs = slice(64 * hp, 64 * hp + 64)
                            if c == 0:
                                t = DVE.op(lambda e: e.tensor_scalar(Sbd[vs, vs], bq[vs, vs], s["fx"][vs, 12:13], None,
                                                                     ALU.mult), tm, s["tfac"], t_c0, *Sbd.free)
                            else:
                                t = DVE.op(lambda e: e.scalar_tensor_tensor(
                                    out=Sbd[vs, vs], in0=bq[vs, vs], scalar=s["fx"][vs, 12 + c:13 + c], in1=Sf[vs, vs],
                                    op0=ALU.mult, op1=ALU.add), tm, tf, ty)
                        t_s = t
                        bq.free = [t]
                    t_y = ACT.op(lambda e: e.activation(YT[:, sl], by[:, 0:128], ACTF.Copy), ty, *YT.free)
                    by.free = [t_y]
                    yield
                Sbd.free = [ty]
                for n in ("Vn", "Kn", "Bn", "Qt"):
                    B2[n].free = [ty]
                G.free = [ty, t_u]
                for hp in range(2):
                    B2[f"RB{hp}"].free = B2[f"RK{hp}"].free = [ty]
                KR.free = s["bt"].free = s["kt"].free = [ty]
                s["fx"].free = [t_s]
                b = bs
                tm = PE.op(lambda e: e.matmul(b[:, :], bd[:, :], YT[:, :], start=True, stop=True), t_y, *b.free)
                t1 = DVE.op(lambda e: e.scalar_tensor_tensor(out=YT[:, :], in0=b[:, :], scalar=-1.0 / 64, in1=YT[:, :],
                                                             op0=ALU.mult, op1=ALU.add), tm, t_y)
                b.free = [t1]
                q = wk2.next()
                t2 = ACT.op(lambda e: e.activation(q[:, :], YT[:, :], ACTF.Square), t1, *q.free)
                yield
                tm = PE.op(lambda e: e.matmul(b[:, :], bd[:, :], q[:, :], start=True, stop=True), t2, *b.free)
                t3 = ACT.op(lambda e: e.activation(q[:, :], b[:, :], ACTF.Sqrt, bias=GEPS, scale=1.0 / 64), tm)
                b.free = [t3]
                yield
                t3 = DVE.op(lambda e: e.reciprocal(q[:, :], q[:, :]), t3)
                t4 = DVE.op(lambda e: e.scalar_tensor_tensor(out=YT[:, :], in0=YT[:, :], scalar=col("gn_gain_2", f),
                                                             in1=q[:, :], op0=ALU.mult, op1=ALU.mult), t3, t1)
                q.free = [t4]
                t5 = DVE.op(lambda e: e.scalar_tensor_tensor(out=YT[:, :], in0=YT[:, :], scalar=col("gn_bias_2", f),
                                                             in1=BO[:, :], op0=ALU.add, op1=ALU.add), t4, s["tbo"])
                BO.free = [t5]
                while f not in gate:
                    yield
                t6 = DVE.op(lambda e: e.tensor_tensor(Y[:, 4 + f, :], YT[:, :], GT[:, :], ALU.mult), t5, gate[f])
                YT.free = GT.free = [t6]
                yt2[4 + f] = t6
                yield

            Y = Z["Y"]
            yt2 = [None] * KT
            gate = {}
            wk2 = Ring([B2["Ww0"], B2["Ww1"]])
            t_hd = None
            pooled = {}

            def pool_u(m, bk, tm):
                b = pads.next()
                t1 = ACT.op(lambda e: e.activation(b[:, 16:], bk[:, :], ACTF.Copy), tm, *b.free)
                bk.free = [t1]
                src, n = b, 1
                others = [pads.next(), pads.next()]
                while n < 2 << m:
                    dst = others[0]
                    others.reverse()
                    t1 = DVE.op(lambda e: e.tensor_tensor(dst[:, 16:], src[:, 16:], src[:, 16 - n:T + 16 - n], ALU.add),
                                t1, *dst.free)
                    src, n = dst, 2 * n
                q = wk.get()
                t2 = DVE.op(lambda e: e.scalar_tensor_tensor(out=q[:, :], in0=src[:, 16:], scalar=1.0 / n, in1=b[:, 16:],
                                                             op0=ALU.mult, op1=ALU.subtract), t1, *q.free)
                t3 = DVE.op(lambda e: e.tensor_tensor(q[:, 0:n - 1], src[:, 16:16 + n - 1], Z["rc"][:, 0:n - 1], ALU.mult),
                            t2)
                t3 = DVE.op(lambda e: e.tensor_tensor(q[:, 0:n - 1], q[:, 0:n - 1], b[:, 16:16 + n - 1], ALU.subtract), t3)
                for x in (b, *others):
                    x.free = [t3]
                pooled[m] = (q, t3)

            def pool_g(m, bk, tm):
                q, tq = pooled[m]
                g = tmp.next()
                t1 = ACT.op(lambda e: e.activation(g[:, :], bk[:, :], ACTF.Silu), tm, *g.free)
                bk.free = [t1]
                b = MB.next()
                tmm = PE.op(lambda e: e.matmul(b[:, :], Z["PW"][:, m * 128:(m + 1) * 128], q[:, :], start=True, stop=True),
                            tq, t_w2, *b.free)
                wk.give(q, tmm)
                yt2[m] = DVE.op(lambda e: e.scalar_tensor_tensor(out=Y[:, m, :], in0=b[:, :], scalar=col("pool_scale_2", m),
                                                                 in1=g[:, :], op0=ALU.mult, op1=ALU.mult), tmm, t1)
                b.free = g.free = [yt2[m]]

            def gate_b(m, bk, tm):
                t = ACT.op(lambda e: e.activation(B2["GT"][:, :], bk[:, :], ACTF.Silu), tm, *B2["GT"].free)
                bk.free = [t]
                gate[m] = t

            side2 = [iter(())]

            late = []

            def step2():
                if late:
                    if next(late[0], done) is done:
                        late.pop()
                next(side2[0], done)

            decays(0)
            for n, m in ORDER2:
                bk, tm = gemm(Hh, Hl, h3, hook=step2)
                t_hd = tm
                if n == "k":
                    late.append(keys(m, bk, tm))
                    next(late[0])
                elif n == "r":
                    receptance(m, bk, tm)
                elif n == "v":
                    if m > 0:
                        for _ in side2[0]:
                            pass
                    values(m, bk, tm)
                    side2[0] = rwkv(m)
                    if m < 3:
                        decays(m + 1)
                elif n == "ua":
                    pool_u(m, bk, tm)
                elif n == "ga":
                    pool_g(m, bk, tm)
                else:
                    gate_b(m, bk, tm)
            y2 = [split(Y[:, m, :], yt2[m], Hh[:, m, :], Hl[:, m, :], [t_hd]) for m in range(KT - 1)]
            for m in range(KT):
                bk, tm = gemm(Hh, Hl, y2, hook=step2, kt=7)
                xt_tok[m] = DVE.op(lambda e: e.tensor_tensor(XT[:, m, :], XT[:, m, :], bk[:, :], ALU.add), tm, xt_tok[m])
                bk.free = [xt_tok[m]]
            for _ in side2[0]:
                pass
            y2.append(split(Y[:, 7, :], yt2[7], Hh[:, 7, :], Hl[:, 7, :], [t_hd]))
            rows = Rows(1)
            i, sl_ = take("w")
            for m in range(KT):
                bk = MB.next()
                PE.wait(*ready[i], *y2[7], *bk.free)
                for w, x in ((whi, Hh), (whi, Hl), (wlo, Hh)):
                    tm = PE.op(lambda e: e.matmul(bk[:, :], w[sl_][:, m, :], x[:, 7, :], start=(w is whi and x is Hh),
                                                  stop=(w is wlo)))
                t1 = DVE.op(lambda e: e.tensor_tensor(XT[:, m, :], XT[:, m, :], bk[:, :], ALU.add), tm, xt_tok[m])
                bk.free = [t1]
                rows.add(m, t1)
                xt_tok[m] = ACT.op(lambda e: e.activation(XT[:, m, :], XT[:, m, :], ACTF.Copy,
                                                          scale=col("final_gain_2", m)), t1, rows.tok[0])
            release(i, tm)
            t_os = rows.rstd(24)
            odead = [y2[-1][0], y2[-1][1], yt2[7]]
        else:
            t_os = DVE.op(lambda e: e.memset(small[:, 24:28], 1.0))
            odead = []

        OT, = region(0, ("OT", [P, 2, D]))
        ofree = [None, None]
        for c in range(NC):
            for q in range(2):
                bk = BK[3 + (2 * c + q) % 4]
                for j in range(4):
                    m = q * 4 + j
                    tt = PE.op(lambda e, m=m, j=j, c=c, bk=bk: e.transpose(bk[:, j * 128:(j + 1) * 128],
                                                                          XT[:, m, c * 128:(c + 1) * 128], ident[:, :]),
                               xt_tok[m], *bk.free)
                to = ACT.op(lambda e, c=c, q=q, bk=bk: e.activation(OT[:, c % 2, q * 512:(q + 1) * 512], bk[:, :],
                                                                   ACTF.Copy, scale=small[:, 24 + c:25 + c]),
                            tt, t_os, ofree[c % 2], *odead)
                bk.free = [to]
            ofree[c % 2] = SP.dma(lambda e, c=c: e.dma_start(out[0, c * 128:(c + 1) * 128, :], OT[:, c % 2, :]),
                                  s_fin[c % 2], 16 * (c // 2 + 1), to)
        SP.wait((s_fin[0], 32), (s_fin[1], 32))


_INS = [
    "x", "c", "w_mod", "b_mod", "w_in", "gm_norm_w", "gm_ws", "gm_bs", "conv_w", "conv_b", "dt_bias", "a_log", "d_skip",
    "ssm_norm_w", "w_branch_gm", "w_branch_ssm", "w_out", "w_ff1", "w_ff2", "final_norm_w", "norm_gain_2",
    "w_in_2", "pool_w_2", "pool_scale_2", "shift_mu_2", "w0_2", "w_up_2", "a0_2", "a_up_2", "k_k_2", "k_a_2", "r_k_2",
    "gn_gain_2", "gn_bias_2", "w_out_2", "final_gain_2",
]
_OUTS = [((1, 512, 1024), "float32")]


def kernel(**inputs):
    import numpy as _np
    import concourse.bacc as _bacc
    from concourse import mybir as _mybir
    from concourse.bass_utils import run_bass_kernel_spmd as _run

    nc = _bacc.Bacc("TRN2", target_bir_lowering=False, num_devices=1)
    arrays, args = {}, {}
    for name in _INS:
        a = _np.ascontiguousarray(inputs[name])
        arrays[f"in_{name}_dram"] = a
        args[name] = nc.dram_tensor(f"in_{name}_dram", a.shape, _mybir.dt.from_np(a.dtype), kind="ExternalInput").ap()
    outs = []
    for i, (shape, dtype) in enumerate(_OUTS):
        dt = _mybir.dt.from_np(_np.dtype(dtype))
        outs.append(nc.dram_tensor(f"out_{i}_dram", shape, dt, kind="ExternalOutput").ap())
    build_program(nc, args, outs[0], BLOCKS)
    r = _run(nc, [arrays], core_ids=[0])
    return r.results[0]["out_0_dram"]
```
